# Optimizing a Trainium2 kernel written in Bass

```python
import math
import jax, jax.numpy as jnp
from jax import lax
import numpy as np

D_MODEL = 1024
BATCH = 1
SEQ = 1024
DEPTH = 1
DEC_BATCH = 8
DEC_SEQ = 4
PAST_LEN = 4096
PAGE_SIZE = 128

MIX_WIDTH = D_MODEL
N_ATT_HEADS = 4
ATT_HEAD_DIM = MIX_WIDTH // (4 * N_ATT_HEADS)
ATT_V_DIM = 2 * ATT_HEAD_DIM
ATT_WIDTH = N_ATT_HEADS * ATT_V_DIM
QK_WIDTH = N_ATT_HEADS * 2 * ATT_HEAD_DIM
CONV_WIDTH = MIX_WIDTH - ATT_WIDTH
CONV_K = 3
PROJ_WIDTH = 2 * QK_WIDTH + ATT_WIDTH + 3 * CONV_WIDTH
NUM_BUCKETS = 32
MAX_DISTANCE = 128
PEER_HEADS = 8
PEER_N_KEYS = 128
PEER_N_EXPERTS = PEER_N_KEYS * PEER_N_KEYS
PEER_TOPK = 16
PEER_KEY_DIM = 256
PEER_HALF = PEER_KEY_DIM // 2
PEER_BLOCK = 128
QUERY_BLOCK = 128
LN_EPS = 1e-5
DEEPNORM_ALPHA = (2.0 * DEPTH) ** 0.25
DEEPNORM_BETA = (8.0 * DEPTH) ** -0.25

kernel_name = "hybrid_diffattn_shortconv_peer_decode_step"

def _layer_norm(x, g, b):
    xf = x.astype(jnp.float32)
    mu = jnp.mean(xf, axis=-1, keepdims=True)
    var = jnp.mean(jnp.square(xf - mu), axis=-1, keepdims=True)
    return ((xf - mu) * lax.rsqrt(var + LN_EPS) * g.astype(jnp.float32) + b.astype(jnp.float32)).astype(x.dtype)

def _adaln(c, w_ada, b_ada):
    m = (jax.nn.silu(c) @ w_ada + b_ada)[:, None, :]
    return jnp.split(m, 6, axis=-1)

def _t5_bucket(dist):
    n = jnp.maximum(dist, 0)
    max_exact = NUM_BUCKETS // 2
    n_large = jnp.maximum(n, max_exact).astype(jnp.float32)
    large = max_exact + (jnp.log(n_large / max_exact) / math.log(MAX_DISTANCE / max_exact)
                         * (NUM_BUCKETS - max_exact)).astype(jnp.int32)
    large = jnp.minimum(large, NUM_BUCKETS - 1)
    return jnp.where(n < max_exact, n, large)

def _diff_lambda(lq1, lk1, lq2, lk2, lam_init):
    f = jnp.float32
    return (jnp.exp(jnp.sum(lq1.astype(f) * lk1.astype(f)))
            - jnp.exp(jnp.sum(lq2.astype(f) * lk2.astype(f))) + lam_init)

def _diff_attention(q, k, v, q_pos, k_pos, rel_bias, lam):
    s = jnp.einsum('bqhmd,bkhmd->bmhqk', q, k,
                   preferred_element_type=jnp.float32) * (ATT_HEAD_DIM ** -0.5)
    dist = q_pos[:, None] - k_pos[None, :]
    bias = jnp.transpose(rel_bias.astype(jnp.float32)[_t5_bucket(dist)], (2, 0, 1))
    s = jnp.where(dist >= 0, s + bias, -jnp.inf)
    p = jax.nn.softmax(s, axis=-1)
    w = p[:, 0] - lam * p[:, 1]
    return jnp.einsum('bhqk,bkhd->bqhd', w.astype(v.dtype), v)

def _diff_post(o, subln_w, lam_init):
    of = o.astype(jnp.float32)
    of = of * lax.rsqrt(jnp.mean(jnp.square(of), axis=-1, keepdims=True) + LN_EPS)
    of = of * subln_w.astype(jnp.float32) * (1.0 - lam_init)
    return of.reshape(o.shape[0], o.shape[1], ATT_WIDTH).astype(o.dtype)

def _prompt_attend(q, k, v, lam, rel_bias):
    b, s = q.shape[0], q.shape[1]
    nqb = s // QUERY_BLOCK
    qb = jnp.moveaxis(q.reshape(b, nqb, QUERY_BLOCK, N_ATT_HEADS, 2, ATT_HEAD_DIM), 1, 0)
    k_pos = jnp.arange(s, dtype=jnp.int32)

    def block(args):
        qi, i = args
        q_pos = i * QUERY_BLOCK + jnp.arange(QUERY_BLOCK, dtype=jnp.int32)
        return _diff_attention(qi, k, v, q_pos, k_pos, rel_bias, lam)

    o = lax.map(block, (qb, jnp.arange(nqb, dtype=jnp.int32)))
    return jnp.moveaxis(o, 0, 1).reshape(b, s, N_ATT_HEADS, ATT_V_DIM)

def _sample_attend(q, k, v, lam, rel_bias, cache_k, cache_v, page_table):
    n_pages = page_table.shape[1]
    past = n_pages * cache_k.shape[1]
    t = q.shape[1]
    q_pos = past + jnp.arange(t, dtype=jnp.int32)
    k_pos = jnp.arange(past + t, dtype=jnp.int32)

    def one(args):
        pt, qi, ki, vi = args
        kp = cache_k[pt].reshape(past, N_ATT_HEADS, 2, ATT_HEAD_DIM)
        vp = cache_v[pt].reshape(past, N_ATT_HEADS, ATT_V_DIM)
        kf = jnp.concatenate([kp, ki.astype(kp.dtype)], axis=0)
        vf = jnp.concatenate([vp, vi.astype(vp.dtype)], axis=0)
        return _diff_attention(qi[None], kf[None], vf[None], q_pos, k_pos, rel_bias, lam)[0]

    return lax.map(one, (page_table, q, k, v))

def _short_conv(gb, gc, hc, prefix, conv_w):
    z = gc * hc
    zf = jnp.concatenate([prefix.astype(z.dtype), z], axis=1)
    s = z.shape[1]
    y = conv_w[0] * zf[:, 0:s] + conv_w[1] * zf[:, 1:s + 1] + conv_w[2] * zf[:, 2:s + 2]
    return gb * y, zf[:, -(CONV_K - 1):]

def _peer(h, w_pq, sub_keys, peer_u, peer_v):
    t, d = h.shape
    nb = -(-t // PEER_BLOCK)
    hp = jnp.pad(h, ((0, nb * PEER_BLOCK - t), (0, 0))).reshape(nb, PEER_BLOCK, d)

    def block(hb):
        q = (hb @ w_pq).reshape(PEER_BLOCK, PEER_HEADS, 2, PEER_HALF)
        s = jnp.einsum('thpd,hpnd->thpn', q, sub_keys, preferred_element_type=jnp.float32)
        sv, si = lax.top_k(s, PEER_TOPK)
        cand = (sv[:, :, 0, :, None] + sv[:, :, 1, None, :]).reshape(
            PEER_BLOCK, PEER_HEADS, PEER_TOPK * PEER_TOPK)
        cv, ci = lax.top_k(cand, PEER_TOPK)
        ea = jnp.take_along_axis(si[:, :, 0], ci // PEER_TOPK, axis=-1)
        eb = jnp.take_along_axis(si[:, :, 1], ci % PEER_TOPK, axis=-1)
        e = ea * PEER_N_KEYS + eb
        g = jax.nn.softmax(cv, axis=-1)
        a = jax.nn.gelu(jnp.einsum('thkd,td->thk', peer_u[e], hb,
                                   preferred_element_type=jnp.float32), approximate=False)
        return jnp.einsum('thk,thkd->td', (g * a).astype(peer_v.dtype), peer_v[e])

    return lax.map(block, hp).reshape(nb * PEER_BLOCK, d)[:t]

def _decoder_layer(x, c, conv_prefix, attend, layer_idx, p):
    lam_init = 0.8 - 0.6 * math.exp(-0.3 * layer_idx)
    b, s, d = x.shape
    shift1, scale1, gate1, shift2, scale2, gate2 = _adaln(c, p['w_ada'], p['b_ada'])
    h = x * (1 + scale1) + shift1
    proj = h @ p['w_in']
    o1 = 2 * QK_WIDTH
    o2 = o1 + ATT_WIDTH
    q = proj[..., :QK_WIDTH].reshape(b, s, N_ATT_HEADS, 2, ATT_HEAD_DIM)
    k = proj[..., QK_WIDTH:o1].reshape(b, s, N_ATT_HEADS, 2, ATT_HEAD_DIM)
    v = proj[..., o1:o2].reshape(b, s, N_ATT_HEADS, ATT_V_DIM)
    gb = proj[..., o2:o2 + CONV_WIDTH]
    gc = proj[..., o2 + CONV_WIDTH:o2 + 2 * CONV_WIDTH]
    hc = proj[..., o2 + 2 * CONV_WIDTH:]
    lam = _diff_lambda(p['lq1'], p['lk1'], p['lq2'], p['lk2'], lam_init)
    o_att = _diff_post(attend(q, k, v, lam), p['subln_w'], lam_init)
    o_conv, conv_state = _short_conv(gb, gc, hc, conv_prefix, p['conv_w'])
    mix = jnp.concatenate([o_att, o_conv], axis=-1) @ p['w_out']
    x = _layer_norm(DEEPNORM_ALPHA * x + gate1 * mix, p['ln1_g'], p['ln1_b'])
    h2 = x * (1 + scale2) + shift2
    f = _peer(h2.reshape(b * s, d), p['w_pq'], p['sub_keys'], p['peer_u'], p['peer_v']).reshape(b, s, d)
    x = _layer_norm(DEEPNORM_ALPHA * x + gate2 * f, p['ln2_g'], p['ln2_b'])
    return x, k, v, conv_state

def setup_inputs(seed: int = 0) -> dict:
    key = jax.random.key(seed)
    ks = jax.random.split(key, 32)
    f = jnp.float32
    D = D_MODEL
    n_pages = PAST_LEN // PAGE_SIZE
    n_used = DEC_BATCH * n_pages
    n_pool = n_used + (n_used + 3) // 4
    page_table = jax.random.permutation(ks[0], n_pool)[:n_used].reshape(DEC_BATCH, n_pages).astype(jnp.int32)
    nrm = lambda k, shape: jax.random.normal(k, shape, f)
    w_in = jnp.concatenate([
        nrm(ks[1], (DEPTH, D, 2 * QK_WIDTH)) * D ** -0.5,
        nrm(ks[2], (DEPTH, D, ATT_WIDTH)) * (D ** -0.5 * DEEPNORM_BETA),
        nrm(ks[3], (DEPTH, D, 3 * CONV_WIDTH)) * D ** -0.5], axis=-1)
    return {
        "x_prompt": nrm(ks[4], (BATCH, SEQ, D)),
        "x_sample": nrm(ks[5], (DEC_BATCH, DEC_SEQ, D)),
        "cache_k": nrm(ks[6], (DEPTH, n_pool, PAGE_SIZE, N_ATT_HEADS, 2, ATT_HEAD_DIM)),
        "cache_v": nrm(ks[7], (DEPTH, n_pool, PAGE_SIZE, N_ATT_HEADS, ATT_V_DIM)),
        "state_conv": nrm(ks[8], (DEPTH, DEC_BATCH, CONV_K - 1, CONV_WIDTH)),
        "page_table": page_table,
        "c_prompt": nrm(ks[9], (BATCH, D)),
        "c_sample": nrm(ks[10], (DEC_BATCH, D)),
        "rel_bias": nrm(ks[11], (NUM_BUCKETS, N_ATT_HEADS)) * 0.5,
        "w_ada": nrm(ks[12], (DEPTH, D, 6 * D)) * D ** -0.5,
        "b_ada": nrm(ks[13], (DEPTH, 6 * D)) * 0.01,
        "w_in": w_in,
        "lambda_q1": nrm(ks[14], (DEPTH, ATT_HEAD_DIM)) * 0.1,
        "lambda_k1": nrm(ks[15], (DEPTH, ATT_HEAD_DIM)) * 0.1,
        "lambda_q2": nrm(ks[16], (DEPTH, ATT_HEAD_DIM)) * 0.1,
        "lambda_k2": nrm(ks[17], (DEPTH, ATT_HEAD_DIM)) * 0.1,
        "subln_w": 1.0 + 0.01 * nrm(ks[18], (DEPTH, ATT_V_DIM)),
        "conv_w": nrm(ks[19], (DEPTH, CONV_K, CONV_WIDTH)) * CONV_K ** -0.5,
        "w_out": nrm(ks[20], (DEPTH, MIX_WIDTH, D)) * (MIX_WIDTH ** -0.5 * DEEPNORM_BETA),
        "ln1_g": 1.0 + 0.01 * nrm(ks[21], (DEPTH, D)),
        "ln1_b": 0.01 * nrm(ks[22], (DEPTH, D)),
        "w_pq": nrm(ks[23], (DEPTH, D, PEER_HEADS * PEER_KEY_DIM)) * D ** -0.5,
        "sub_keys": nrm(ks[24], (DEPTH, PEER_HEADS, 2, PEER_N_KEYS, PEER_HALF)) * PEER_HALF ** -0.5,
        "peer_u": nrm(ks[25], (DEPTH, PEER_N_EXPERTS, D)) * (D ** -0.5 * DEEPNORM_BETA),
        "peer_v": nrm(ks[26], (DEPTH, PEER_N_EXPERTS, D)) * DEEPNORM_BETA,
        "ln2_g": 1.0 + 0.01 * nrm(ks[27], (DEPTH, D)),
        "ln2_b": 0.01 * nrm(ks[28], (DEPTH, D)),
    }

def reference(x_prompt, x_sample, cache_k, cache_v, state_conv, page_table, c_prompt, c_sample,
              rel_bias, w_ada, b_ada, w_in, lambda_q1, lambda_k1, lambda_q2, lambda_k2, subln_w,
              conv_w, w_out, ln1_g, ln1_b, w_pq, sub_keys, peer_u, peer_v, ln2_g, ln2_b):
    y_prompt, y_sample = x_prompt, x_sample
    kp_list, vp_list, cp_list, ks_list, vs_list, cs_list = [], [], [], [], [], []
    zero_prefix = jnp.zeros((x_prompt.shape[0], CONV_K - 1, CONV_WIDTH), x_prompt.dtype)
    for layer in range(DEPTH):
        p = dict(w_ada=w_ada[layer], b_ada=b_ada[layer], w_in=w_in[layer],
                 lq1=lambda_q1[layer], lk1=lambda_k1[layer], lq2=lambda_q2[layer], lk2=lambda_k2[layer],
                 subln_w=subln_w[layer], conv_w=conv_w[layer], w_out=w_out[layer],
                 ln1_g=ln1_g[layer], ln1_b=ln1_b[layer], w_pq=w_pq[layer], sub_keys=sub_keys[layer],
                 peer_u=peer_u[layer], peer_v=peer_v[layer], ln2_g=ln2_g[layer], ln2_b=ln2_b[layer])
        ck, cv = cache_k[layer], cache_v[layer]
        attend_prompt = lambda q, k, v, lam: _prompt_attend(q, k, v, lam, rel_bias)
        attend_sample = lambda q, k, v, lam: _sample_attend(q, k, v, lam, rel_bias, ck, cv, page_table)
        y_prompt, kp, vp, cp = _decoder_layer(y_prompt, c_prompt, zero_prefix, attend_prompt, layer, p)
        y_sample, ksn, vsn, csn = _decoder_layer(y_sample, c_sample, state_conv[layer], attend_sample, layer, p)
        kp_list.append(kp)
        vp_list.append(vp)
        cp_list.append(cp)
        ks_list.append(ksn)
        vs_list.append(vsn)
        cs_list.append(csn)
    new_k_prompt = jnp.stack(kp_list)
    new_v_prompt = jnp.stack(vp_list)
    new_conv_prompt = jnp.stack(cp_list)
    new_k_sample = jnp.stack(ks_list)
    new_v_sample = jnp.stack(vs_list)
    new_conv_sample = jnp.stack(cs_list)
    return (y_prompt, y_sample, new_k_prompt, new_v_prompt, new_conv_prompt, new_k_sample, new_v_sample, new_conv_sample)


_drawn_inputs = setup_inputs


def setup_inputs(seed=0):
    import zlib

    import numpy as np

    out = dict(_drawn_inputs(seed))
    spreads = {}
    factors = {'b_ada': 3.273,
     'lambda_q1': 200.0,
     'lambda_k1': 2.969,
     'subln_w': 47.842,
     'ln1_g': 16.087,
     'ln1_b': 16.759,
     'ln2_g': 200.0,
     'ln2_b': 200.0}
    for name, (base, spread) in spreads.items():
        noise = np.random.default_rng([zlib.crc32(name.encode()), seed]).standard_normal(out[name].shape)
        drawn = base * np.exp(spread * noise) if base else spread * noise
        out[name] = __import__('jax').numpy.asarray(drawn.astype(out[name].dtype))
    for name, factor in factors.items():
        out[name] = (out[name] * factor).astype(out[name].dtype)
    return out
```

```python
import math
from contextlib import ExitStack

import numpy as np

import concourse.bass as bass
from concourse import mybir

F32 = mybir.dt.float32
U32 = mybir.dt.uint32
I32 = mybir.dt.int32
ALU = mybir.AluOpType
ACT = mybir.ActivationFunctionType
AX = mybir.AxisListType.X
ds = bass.ds

P = 128
D = 1024
KD = D // P
SEQ = 1024
TILES = SEQ // P
NB, NT = 8, 4
NS = NB * NT
NC = 1 + NB
H, DH, DV = 4, 64, 128
AW = H * DV
PAGES = 32
POOL = 320
PAST = PAGES * P
CONV = 3
BUCKETS, MAX_DIST = 32, 128
PH, PK, TOPK = 8, 128, 16
HP = 2 * PH
SEL = PH * TOPK
ALPHA = 2.0 ** 0.25
EPS = 1e-5
LAM_INIT = 0.8 - 0.6 * math.exp(-0.3 * 0)
MASKED = -1e30
BANK = 512
STRIP = SEQ + BANK
TOEP = STRIP + P - 1
TAIL = P + NT
SHIFT1, SCALE1, GATE1, SHIFT2, SCALE2, GATE2 = range(6)
GROUP = 4
RING = 8


def take(eng, sem, n=1):
    eng.wait_ge(sem, n)
    eng.sem_inc(sem, -n)


class Steps:

    def __init__(self, eng, sem):
        self.eng, self.sem, self.n = eng, sem, 0

    def __call__(self, ins):
        ins.then_inc(self.sem, 1)
        self.n += 1

    def done(self):
        self.eng.wait_ge(self.sem, self.n)

    def reset(self):
        if self.n:
            self.done()
            self.eng.sem_inc(self.sem, -self.n)
            self.n = 0

    def tell(self, *sems):
        self.done()
        for s in sems:
            self.eng.sem_inc(s, 1)


def flat(ap):
    return ap.rearrange("p a n -> p (a n)")


def over(ap, n):
    return ap.unsqueeze(2).to_broadcast([ap.shape[0], ap.shape[1], n])


def build(nc, A):
    with ExitStack() as top:
        used = []

        def sem(name):
            used.append(nc.alloc_semaphore(name=name))
            return used[-1]

        def end_stage():
            nc.clear_and_free_semaphores(used)
            nc.all_engine_barrier()
            used.clear()

        def sbuf(stack, name, shape, dt=F32):
            return stack.enter_context(nc.sbuf_tensor("sb_" + name, shape, dt))

        psum = top.enter_context(nc.psum_tensor("psum", [P, 8, BANK], F32))
        toep_dram = nc.dram_tensor("toep_scratch", (H, P, TOEP), F32, kind="Internal").ap()
        x1_dram = nc.dram_tensor("x1_scratch", (SEQ + P, D), F32, kind="Internal").ap()
        mod_dram = nc.dram_tensor("mod_scratch", (NC, 6 * D), F32, kind="Internal").ap()
        h2_dram = nc.dram_tensor("h2_scratch", (SEQ + P, D), F32, kind="Internal").ap()

        ident = sbuf(top, "ident", [P, P])
        ones = sbuf(top, "ones", [P, P])
        gate2 = sbuf(top, "gate2", [P, 2, D])
        lam = sbuf(top, "lam", [P, 2])
        eps = sbuf(top, "eps", [P, 1])
        tensors = dict(nc=nc, A=A, sem=sem, sbuf=sbuf, psum=psum, toep_dram=toep_dram, x1_dram=x1_dram,
                       h2_dram=h2_dram, mod_dram=mod_dram, ident=ident, ones=ones, lam=lam, eps=eps, gate2=gate2)
        with ExitStack() as mid:
            tensors |= dict(sel=sbuf(mid, "sel", [NC, 2, P]), modT=sbuf(mid, "modT", [P, 2, KD, NC]))
            condition(**tensors)
            end_stage()
            o_att = sbuf(mid, "o_att", [P, TILES + 1, AW])
            o_convT = sbuf(mid, "o_convT", [P, H, SEQ + NS])
            tensors |= dict(o_att=o_att, o_convT=o_convT)
            with ExitStack() as att:
                tensors |= dict(qT=sbuf(att, "qT", [P, H, SEQ + NS]), kT=sbuf(att, "kT", [P, H, SEQ + NS]),
                                v=sbuf(att, "v", [P, TILES + 1, AW]))
                project(**tensors)
                end_stage()
                prompt_attention(**tensors)
                end_stage()
                sample_attention(**tensors)
                end_stage()
            mix(**tensors)
            end_stage()
        peer(**tensors)


def condition(nc, A, sem, sbuf, psum, mod_dram, ident, sel, ones, modT, lam, eps, **_):
    NBLK, SL = 12, 3
    with ExitStack() as st:
        w = sbuf(st, "w_ada", [P, SL, KD, BANK])
        b = sbuf(st, "b_ada", [1, SL, BANK])
        mod = sbuf(st, "mod", [NC, 6 * D])
        c = sbuf(st, "c", [NC, D])
        cs = sbuf(st, "c_silu", [NC, D])
        cT = sbuf(st, "cT", [P, KD, NC])
        lq = sbuf(st, "lq", [1, 4, DH])
        lw = sbuf(st, "lw", [1, 8])
        consts, w_land, w_free = sem("consts"), [sem(f"w_ada_land{u}") for u in range(SL)], [sem(f"w_ada_free{u}") for u in range(SL)]
        silu, cT_psum, cT_sbuf = sem("silu"), sem("cT_psum"), sem("cT_sbuf")
        m_psum, m_free = [sem(f"m_psum{u}") for u in range(2)], [sem(f"m_free{u}") for u in range(2)]
        mod_ready, modT_psum, lam_exp, lam_arg, lam_bc, lam_row = (sem("mod_ready"), sem("modT_psum"), sem("lam_exp"),
                                                                  sem("lam_arg"), sem("lam_bc"), sem("lam_row"))
        dve_c, act_c, ones_ready, mod_stored = sem("dve_c"), sem("act_c"), sem("ones_ready"), sem("mod_stored")
        w_v = A["w_ada"][0].rearrange("(k p) n -> p k n", p=P)
        with nc.Block() as block:
            @block.sync
            def _(sp):
                sp.dma_start(c[0:1, :], A["c_prompt"]).then_inc(consts, 16)
                sp.dma_start(c[1:NC, :], A["c_sample"]).then_inc(consts, 16)
                sp.dma_start(ident[:], A["const_ident"]).then_inc(consts, 16)
                sp.dma_start(sel[:], A["const_sel"]).then_inc(consts, 16)
                for n, name in enumerate(("lambda_q1", "lambda_k1", "lambda_q2", "lambda_k2")):
                    sp.dma_start(lq[:, n, :], A[name]).then_inc(consts, 16)
                with sp.Fori(0, NBLK // SL) as i:
                    for u in range(SL):
                        take(sp, w_free[u])
                        sp.dma_start(w[:, u], w_v[:, :, ds((i * SL + u) * BANK, BANK)]).then_inc(w_land[u], 16)
                        sp.dma_start(b[:, u, :], A["b_ada"][:, ds((i * SL + u) * BANK, BANK)]).then_inc(w_land[u], 16)
                sp.wait_ge(mod_ready, 1)
                sp.dma_start(mod_dram, mod[:]).then_inc(mod_stored, 16)
                sp.wait_ge(mod_stored, 16)

            @block.scalar
            def _(act):
                act.wait_ge(consts, 8 * 16)
                nc.scalar.activation(cs[:], c[:], ACT.Silu).then_inc(silu, 1)
                act.wait_ge(cT_psum, 1)
                nc.scalar.copy(cT[:], psum[:, 2, 0:KD * NC].rearrange("p (k c) -> p k c", k=KD)).then_inc(cT_sbuf, 1)
                with act.Fori(0, NBLK // 6) as i:
                    for n in range(6):
                        take(act, m_psum[n % 2])
                        act.sem_inc(w_free[n % SL], 1)
                        nc.scalar.copy(mod[:, ds((i * 6 + n) * BANK, BANK)], psum[0:NC, n % 2, :]).then_inc(m_free[n % 2], 1)
                act.wait_ge(lam_arg, 1)
                nc.scalar.activation(lw[:, 2:4], lw[:, 0:2], ACT.Exp).then_inc(lam_exp, 1)

            @block.tensor
            def _(pe):
                pe.wait_ge(consts, 8 * 16)
                pe.wait_ge(silu, 1)
                for k in range(KD):
                    ins = nc.tensor.transpose(psum[:, 2, k * NC:(k + 1) * NC], cs[:, k * P:(k + 1) * P], ident[0:NC, 0:NC])
                ins.then_inc(cT_psum, 1)
                pe.wait_ge(cT_sbuf, 1)
                pe.wait_ge(ones_ready, 1)
                for u in range(SL):
                    pe.sem_inc(w_free[u], 1)
                for u in range(2):
                    pe.sem_inc(m_free[u], 1)
                with pe.Fori(0, NBLK // 6) as i:
                    for n in range(6):
                        u, m = n % SL, n % 2
                        take(pe, w_land[u], 32)
                        take(pe, m_free[m])
                        for k in range(KD):
                            nc.tensor.matmul(psum[0:NC, m, :], cT[:, k, :], w[:, u, k, :], start=(k == 0), stop=False)
                        nc.tensor.matmul(psum[0:NC, m, :], ones[0:1, 0:NC], b[:, u, :],
                                         start=False, stop=True).then_inc(m_psum[m], 1)
                for m in range(2):
                    take(pe, m_free[m])
                pe.sem_inc(mod_ready, 1)
                for q, kind in enumerate((SHIFT1, SCALE1)):
                    for k in range(KD):
                        ins = nc.tensor.transpose(psum[:, 3, (q * KD + k) * NC:(q * KD + k + 1) * NC],
                                                  mod[:, kind * D + k * P:kind * D + (k + 1) * P], ident[0:NC, 0:NC])
                ins.then_inc(modT_psum, 1)
                pe.wait_ge(lam_row, 1)
                nc.tensor.matmul(psum[:, 4, 0:1], ones[0:1, :], lw[:, 4:5], start=True, stop=True).then_inc(lam_bc, 1)

            @block.vector
            def _(dve):
                step = Steps(dve, dve_c)
                step(nc.vector.memset(ones[:], 1.0))
                step(nc.vector.memset(eps[:], EPS))
                step.tell(ones_ready)
                dve.wait_ge(consts, 8 * 16)
                for n in range(2):
                    step(nc.vector.tensor_tensor_reduce(lq[:, 2 * n, :], lq[:, 2 * n, :], lq[:, 2 * n + 1, :], 1.0, 0.0,
                                                        ALU.mult, ALU.add, lw[:, n:n + 1]))
                step.tell(lam_arg)
                dve.wait_ge(lam_exp, 1)
                step(nc.vector.tensor_tensor(lw[:, 5:6], lw[:, 2:3], lw[:, 3:4], ALU.subtract))
                step.done()
                step(nc.vector.tensor_scalar(lw[:, 4:5], lw[:, 5:6], LAM_INIT, None, ALU.add))
                step.tell(lam_row)
                dve.wait_ge(modT_psum, 1)
                for q in range(2):
                    step(nc.vector.tensor_scalar(modT[:, q], psum[:, 3, q * KD * NC:(q + 1) * KD * NC].rearrange(
                        "p (k c) -> p k c", k=KD), float(q % 2), None, ALU.add))
                dve.wait_ge(lam_bc, 1)
                step(nc.vector.tensor_copy(lam[:, 0:1], psum[:, 4, 0:1]))
                step(nc.vector.tensor_scalar(lam[:, 1:2], psum[:, 4, 0:1], -1.0, None, ALU.mult))
                step.done()


def project(nc, A, sem, sbuf, psum, ident, modT, qT, kT, v, o_convT, **_):
    with ExitStack() as outer, ExitStack() as st:
        hT = sbuf(outer, "hT", [P, KD, SEQ + NS])
        w = sbuf(st, "w_qkv", [P, KD, 3 * AW])
        x = sbuf(st, "x_in", [P, 2, D])
        hTt = sbuf(st, "hT_tile", [P, 2, KD, P])
        qk = sbuf(st, "qk_tile", [P, 2, 2 * AW])
        vo = sbuf(st, "v_tile", [P, 2, AW])
        names = ["w_land", "hT_last", "conv_done"]
        S = {n: sem("pj_" + n) for n in names}
        D2 = {n: [sem(f"pj_{n}{u}") for u in range(2)] for n in
              ("x_land", "x_free", "xT_ready", "hT_ready", "hT_free", "proj_ready", "qk_ready", "stored", "qkT_psum",
               "xT_free", "qkT_free", "proj_free", "qk_free")}
        act_c, dve_c = sem("pj_act_c"), sem("pj_dve_c")
        w_v = A["w_in"][0].rearrange("(k p) n -> p k n", p=P)
        x_t = A["x_prompt"][0].rearrange("(t p) d -> p t d", p=P)
        k_out = A["new_k_prompt"][0, 0].rearrange("(t p) h m d -> p t (h m d)", p=P)
        v_out = A["new_v_prompt"][0, 0].rearrange("(t p) h d -> p t (h d)", p=P)
        ks_out = A["new_k_sample"][0].rearrange("b t h m d -> (b t) (h m d)")
        vs_out = A["new_v_sample"][0].rearrange("b t h d -> (b t) (h d)")
        xs = A["x_sample"].rearrange("b t d -> (b t) d")

        def tiles(eng, body):
            with eng.Fori(0, TILES // 2) as i:
                for u in range(2):
                    body(u, i * 2 + u)
            body(0, None)

        with nc.Block() as block:
            @block.sync
            def _(sp):
                sp.dma_start(w[:, :, 0:2 * AW], w_v[:, :, 0:2 * AW]).then_inc(S["w_land"], 16)
                sp.dma_start(w[:, :, 2 * AW:3 * AW], w_v[:, :, 2 * AW:3 * AW]).then_inc(S["w_land"], 16)

                def body(u, t):
                    take(sp, D2["x_free"][u])
                    if t is None:
                        sp.dma_start(x[0:NS, u, :], xs).then_inc(D2["x_land"][u], 16)
                    else:
                        sp.dma_start(x[:, u, :], flat(x_t[:, ds(t, 1), :])).then_inc(D2["x_land"][u], 16)
                tiles(sp, body)

            @block.tensor
            def _(pe):
                for u in range(2):
                    pe.sem_inc(D2["x_free"][u], 1)
                pe.wait_ge(S["w_land"], 32)

                def body(u, t):
                    n = NS if t is None else P
                    take(pe, D2["x_land"][u], 16)
                    take(pe, D2["xT_free"][0])
                    for k in range(KD):
                        ins = nc.tensor.transpose(psum[:, k // 4, (k % 4) * P:(k % 4) * P + n],
                                                  x[0:n, u, k * P:(k + 1) * P], ident[0:n, 0:n])
                    ins.then_inc(D2["xT_ready"][0], 1)
                    take(pe, D2["hT_ready"][u])
                    for j in range(3):
                        take(pe, D2["proj_free"][0])
                        for k in range(KD):
                            ins = nc.tensor.matmul(psum[0:n, 2 + j, :], hTt[:, u, k, 0:n], w[:, k, j * AW:(j + 1) * AW],
                                                   start=(k == 0), stop=(k == KD - 1))
                        ins.then_inc(D2["proj_ready"][0], 1)
                    take(pe, D2["qk_ready"][u])
                    take(pe, D2["qkT_free"][0])
                    for j in range(2 * H):
                        ins = nc.tensor.transpose(psum[:, 5 + j // 4, (j % 4) * P:(j % 4) * P + n],
                                                  qk[0:n, u, j * P:(j + 1) * P], ident[0:n, 0:n])
                    ins.then_inc(D2["qkT_psum"][0], 1)
                tiles(pe, body)

            @block.scalar
            def _(act):
                step = Steps(act, act_c)
                act.sem_inc(D2["qkT_free"][0], 1)
                act.sem_inc(D2["proj_free"][0], 3)

                def body(u, t):
                    n = NS if t is None else P
                    at = SEQ if t is None else t * P
                    for j in range(3):
                        take(act, D2["proj_ready"][0])
                        if j == 0:
                            take(act, D2["stored"][u], 32)
                        if j < 2:
                            step(nc.scalar.copy(qk[0:n, u, j * AW:(j + 1) * AW], psum[0:n, 2 + j, :]))
                        else:
                            step(nc.scalar.copy(vo[0:n, u, :], psum[0:n, 2 + j, :]))
                        step.tell(D2["proj_free"][0])
                        if j == 1:
                            act.sem_inc(D2["qk_ready"][u], 1)
                    if t is None:
                        act.dma_start(ks_out, qk[0:NS, u, AW:2 * AW]).then_inc(D2["stored"][u], 16)
                        act.dma_start(vs_out, vo[0:NS, u, :]).then_inc(D2["stored"][u], 16)
                        step(nc.scalar.copy(v[0:NS, TILES, :], vo[0:NS, u, :]))
                    else:
                        act.dma_start(flat(k_out[:, ds(t, 1), :]), qk[:, u, AW:2 * AW]).then_inc(D2["stored"][u], 16)
                        act.dma_start(flat(v_out[:, ds(t, 1), :]), vo[:, u, :]).then_inc(D2["stored"][u], 16)
                        step(nc.scalar.copy(flat(v[:, ds(t, 1), :]), vo[:, u, :]))
                    take(act, D2["qkT_psum"][0])
                    src = psum[:, 5:7, :].rearrange("p b (h n) -> p b h n", h=H)
                    step(nc.scalar.mul(qT[:, :, ds(at, n)], src[:, 0, :, 0:n], DH ** -0.5))
                    step(nc.scalar.copy(kT[:, :, ds(at, n)], src[:, 1, :, 0:n]))
                    step.tell(D2["qkT_free"][0])
                    step.reset()

                for u in range(2):
                    act.sem_inc(D2["stored"][u], 32)
                tiles(act, body)
                for u in range(2):
                    act.wait_ge(D2["stored"][u], 32)

            @block.vector
            def _(dve):
                step = Steps(dve, dve_c)
                dve.sem_inc(D2["xT_free"][0], 1)

                def body(u, t):
                    take(dve, D2["xT_ready"][0])
                    if t is not None:
                        for k in range(KD):
                            src = psum[:, k // 4, (k % 4) * P:(k % 4 + 1) * P]
                            step(nc.vector.tensor_scalar(hTt[:, u, k, :], src, modT[:, 1, k, 0:1], modT[:, 0, k, 0:1],
                                                         ALU.mult, ALU.add))
                        step.tell(D2["hT_ready"][u], D2["xT_free"][0], D2["x_free"][u])
                        step(nc.vector.tensor_copy(hT[:, :, ds(t * P, P)], hTt[:, u]))
                    else:
                        for k in range(KD):
                            src = psum[:, k // 4, (k % 4) * P:(k % 4) * P + NS].rearrange("p (b t) -> p b t", t=NT)
                            dst = hTt[:, u, k, 0:NS].rearrange("p (b t) -> p b t", t=NT)
                            step(nc.vector.tensor_tensor(dst, src, over(modT[:, 1, k, 1:NC], NT), ALU.mult))
                        step.done()
                        for k in range(KD):
                            dst = hTt[:, u, k, 0:NS].rearrange("p (b t) -> p b t", t=NT)
                            step(nc.vector.tensor_tensor(dst, dst, over(modT[:, 0, k, 1:NC], NT), ALU.add))
                        step.tell(D2["hT_ready"][u], D2["xT_free"][0])
                        step(nc.vector.tensor_copy(hT[:, :, SEQ:SEQ + NS], hTt[:, u, :, 0:NS]))
                    step.reset()
                tiles(dve, body)

        st.close()
        conv(nc, A, sem, sbuf, psum, hT, o_convT)


def conv(nc, A, sem, sbuf, psum, hT, o_convT):
    with ExitStack() as st:
        w = sbuf(st, "w_bcu", [P, 3, KD, P])
        cw = sbuf(st, "conv_w", [P, H, CONV])
        cwc = sbuf(st, "conv_w_now", [P, CONV])
        pre = sbuf(st, "conv_prefix", [P, H, NB, 2])
        gc = sbuf(st, "gate_c", [P, SEQ + NS])
        z = sbuf(st, "z", [P, 2 + SEQ])
        zs = sbuf(st, "z_sample", [P, NB, 2 + NT])
        y = sbuf(st, "conv_y", [P, SEQ + NS])
        zlast = sbuf(st, "z_last", [P, H, 2])
        zslast = sbuf(st, "z_sample_last", [P, H, NB, 2])
        land, free = [sem(f"cv_w_land{j}") for j in range(3)], [sem(f"cv_w_free{j}") for j in range(3)]
        small, stored = sem("cv_small"), sem("cv_stored")
        psum_ready, psum_free, gc_ready, gc_free = sem("cv_psum_ready"), sem("cv_psum_free"), sem("cv_gc_ready"), sem("cv_gc_free")
        last_ready, dve_c, act_c = sem("cv_last_ready"), sem("cv_dve"), sem("cv_act")
        w_v = A["w_in"][0].rearrange("(k p) n -> p k n", p=P)
        PARTS = ((0, BANK), (BANK, BANK), (SEQ, NS))
        COL = (4 * AW, 5 * AW, 3 * AW)

        def where(part, j):
            return psum[:, 3 * part + j, :] if part < 2 else psum[:, 6, j * NS:(j + 1) * NS]

        with nc.Block() as block:
            @block.sync
            def _(sp):
                with nc.allow_non_contiguous_dma("small"):
                    for j in range(CONV):
                        sp.dma_start(cw[:, :, j], A["conv_w"][0, j].rearrange("(c p) -> p c", p=P)).then_inc(small, 16)
                    for b in range(NB):
                        for r in range(2):
                            sp.dma_start(pre[:, :, b, r], A["state_conv"][0, b, r].rearrange("(c p) -> p c", p=P)).then_inc(small, 16)
                with sp.Fori(0, H) as c:
                    for j in range(3):
                        take(sp, free[j])
                        sp.dma_start(w[:, j], w_v[:, :, ds(c * P + COL[j], P)]).then_inc(land[j], 16)
                sp.wait_ge(last_ready, 1)
                with nc.allow_non_contiguous_dma("small"):
                    for r in range(2):
                        sp.dma_start(A["new_conv_prompt"][0, 0, r].rearrange("(c p) -> p c", p=P), zlast[:, :, r]).then_inc(stored, 16)
                        for b in range(NB):
                            sp.dma_start(A["new_conv_sample"][0, b, r].rearrange("(c p) -> p c", p=P),
                                         zslast[:, :, b, r]).then_inc(stored, 16)
                sp.wait_ge(stored, 16 * 2 * (1 + NB))

            @block.tensor
            def _(pe):
                for j in range(3):
                    pe.sem_inc(free[j], 1)
                with pe.Fori(0, H) as c:
                    for part, (at, n) in enumerate(PARTS):
                        take(pe, psum_free)
                        for j in range(3):
                            if part == 0:
                                take(pe, land[j], 16)
                            for k in range(KD):
                                ins = nc.tensor.matmul(where(part, j), w[:, j, k, :], hT[:, k, at:at + n],
                                                       start=(k == 0), stop=(k == KD - 1))
                        ins.then_inc(psum_ready, 1)

            @block.scalar
            def _(act):
                with act.Fori(0, H) as c:
                    for part, (at, n) in enumerate(PARTS):
                        take(act, psum_ready)
                        if part == 2:
                            for j in range(3):
                                act.sem_inc(free[j], 1)
                        take(act, gc_free)
                        nc.scalar.copy(gc[:, at:at + n], where(part, 0)).then_inc(gc_ready, 1)

            @block.vector
            def _(dve):
                step = Steps(dve, dve_c)
                dve.sem_inc(psum_free, 3)
                dve.sem_inc(gc_free, 3)
                dve.wait_ge(small, 16 * (CONV + 2 * NB))
                step(nc.vector.memset(z[:, 0:2], 0.0))
                step.reset()
                with dve.Fori(0, H) as c:
                    step(nc.vector.tensor_copy(cwc[:], flat(cw[:, ds(c, 1), :])))
                    step(nc.vector.tensor_copy(zs[:, :, 0:2], pre[:, ds(c, 1)].rearrange("p a b r -> p (a b) r")))
                    for part, (at, n) in enumerate(PARTS):
                        take(dve, gc_ready)
                        if part < 2:
                            new, y_p = z[:, 2 + at:2 + at + n], y[:, at:at + n]
                            gc_p, u_p, b_p = gc[:, at:at + n], where(part, 1), where(part, 2)
                            old = [z[:, at + j:at + j + n] for j in range(CONV)]
                        else:
                            split = lambda ap: ap.rearrange("p (b t) -> p b t", t=NT)
                            new, y_p = zs[:, :, 2:], split(y[:, at:at + n])
                            gc_p, u_p, b_p = split(gc[:, at:at + n]), split(where(2, 1)), split(where(2, 2))
                            old = [zs[:, :, j:j + NT] for j in range(CONV)]
                        step(nc.vector.tensor_tensor(new, gc_p, u_p, ALU.mult))
                        step.done()
                        step(nc.vector.tensor_scalar(y_p, old[0], cwc[:, 0:1], None, ALU.mult))
                        for j in (1, 2):
                            step.done()
                            step(nc.vector.scalar_tensor_tensor(out=y_p, in0=old[j], scalar=cwc[:, j:j + 1], in1=y_p,
                                                                op0=ALU.mult, op1=ALU.add))
                        step.done()
                        dst = o_convT[:, ds(c, 1), at:at + n].rearrange("p a n -> p (a n)")
                        step(nc.vector.tensor_tensor(dst if part < 2 else dst.rearrange("p (b t) -> p b t", t=NT),
                                                     y_p, b_p, ALU.mult))
                        step.tell(psum_free, gc_free)
                    step(nc.vector.tensor_copy(flat(zlast[:, ds(c, 1), :]), z[:, SEQ:SEQ + 2]))
                    step(nc.vector.tensor_copy(zslast[:, ds(c, 1)].rearrange("p a b r -> p (a b) r"), zs[:, :, NT:NT + 2]))
                    step.reset()
                dve.sem_inc(last_ready, 1)


def prompt_attention(nc, A, sem, sbuf, psum, toep_dram, ident, ones, lam, qT, kT, v, o_att, **_):
    with ExitStack() as st:
        strip = sbuf(st, "strip", [P, H, STRIP])
        toeplitz(nc, A, sem, sbuf, psum, toep_dram, strip)
        q_now = sbuf(st, "q_now", [P, H, P])
        bias = sbuf(st, "bias_now", [P, H, SEQ])
        e = sbuf(st, "scores", [P, 2, 2, SEQ])
        wgt = sbuf(st, "weights", [P, SEQ])
        wT = sbuf(st, "weightsT", [P, TILES, P])
        mx, nmx = sbuf(st, "row_max", [P, 2, 2]), sbuf(st, "neg_max", [P, 2, 2])
        z, rz = sbuf(st, "row_sum", [P, 2, 2]), sbuf(st, "row_scale", [P, 2])
        names = ("staged_pe staged_dve stage_free s_ready s_free e_ready p_ready w_ready w_free wT_psum wT_free wT_ready "
                 "o_ready o_free").split()
        T = {n: sem("at_" + n) for n in names}
        dve_c, act_c, pool_c = sem("at_dve"), sem("at_act"), sem("at_pool")

        def tiles(eng, body):
            for nb in (1, 2):
                with eng.Fori(0, TILES // 2) as i:
                    body(i + (nb - 1) * (TILES // 2), nb)

        with nc.Block() as block:
            @block.gpsimd
            def _(pool):
                step = Steps(pool, pool_c)

                def body(t, nb):
                    take(pool, T["stage_free"])
                    step(nc.gpsimd.tensor_copy(q_now[:], qT[:, :, ds(t * P, P)]))
                    step(nc.gpsimd.tensor_copy(bias[:, :, 0:nb * BANK], strip[:, :, ds(SEQ - t * P, nb * BANK)]))
                    step.tell(T["staged_pe"], T["staged_dve"])
                    step.reset()
                tiles(pool, body)

            @block.tensor
            def _(pe):
                pe.sem_inc(T["s_free"], 1)
                pe.sem_inc(T["w_free"], 1)
                pe.sem_inc(T["wT_free"], 1)
                pe.sem_inc(T["o_free"], 1)

                def scores(h, nb):
                    take(pe, T["s_free"])
                    for m in range(2):
                        for b in range(nb):
                            ins = nc.tensor.matmul(psum[:, 2 * m + b, :], q_now[m * DH:(m + 1) * DH, h, :],
                                                   kT[m * DH:(m + 1) * DH, h, b * BANK:(b + 1) * BANK], start=True, stop=True)
                    ins.then_inc(T["s_ready"], 1)

                def values(h, nb):
                    take(pe, T["w_ready"])
                    take(pe, T["wT_free"])
                    for j in range(4 * nb):
                        ins = nc.tensor.transpose(psum[:, 4 + j // 4, (j % 4) * P:(j % 4 + 1) * P],
                                                  wgt[:, j * P:(j + 1) * P], ident[:])
                    ins.then_inc(T["wT_psum"], 1)
                    take(pe, T["wT_ready"])
                    if h == 0:
                        take(pe, T["o_free"])
                    for j in range(4 * nb):
                        ins = nc.tensor.matmul(psum[:, 6, h * DV:(h + 1) * DV], wT[:, j, :], v[:, j, h * DV:(h + 1) * DV],
                                               start=(j == 0), stop=(j == 4 * nb - 1))
                    if h == H - 1:
                        ins.then_inc(T["o_ready"], 1)

                def body(t, nb):
                    take(pe, T["staged_pe"])
                    scores(0, nb)
                    for h in range(H):
                        if h + 1 < H:
                            scores(h + 1, nb)
                        values(h, nb)
                tiles(pe, body)

            @block.vector
            def _(dve):
                step = Steps(dve, dve_c)
                dve.sem_inc(T["stage_free"], 1)

                def biased(h, nb):
                    take(dve, T["s_ready"])
                    u = h % 2
                    for m in range(2):
                        step(nc.vector.tensor_tensor_reduce(
                            e[:, u, m, 0:nb * BANK], flat(psum[:, 2 * m:2 * m + nb, :]), bias[:, h, 0:nb * BANK], 1.0, MASKED,
                            ALU.add, ALU.max, mx[:, u, m:m + 1]))
                    step.done()
                    step(nc.vector.tensor_scalar(nmx[:, u, :], mx[:, u, :], -1.0, None, ALU.mult))
                    step.tell(T["e_ready"], T["s_free"])
                    if h == H - 1:
                        dve.sem_inc(T["stage_free"], 1)

                def combined(h, nb):
                    take(dve, T["p_ready"])
                    u = h % 2
                    step(nc.vector.reciprocal(rz[:], z[:, u, :]))
                    step.done()
                    step(nc.vector.tensor_tensor(rz[:, 1:2], rz[:, 1:2], lam[:, 1:2], ALU.mult))
                    step.done()
                    step(nc.vector.tensor_scalar(e[:, u, 1, 0:nb * BANK], e[:, u, 1, 0:nb * BANK], rz[:, 1:2], None, ALU.mult))
                    step.done()
                    take(dve, T["w_free"])
                    step(nc.vector.scalar_tensor_tensor(out=wgt[:, 0:nb * BANK], in0=e[:, u, 0, 0:nb * BANK], scalar=rz[:, 0:1],
                                                        in1=e[:, u, 1, 0:nb * BANK], op0=ALU.mult, op1=ALU.add))
                    step.tell(T["w_ready"])

                def body(t, nb):
                    take(dve, T["staged_dve"])
                    biased(0, nb)
                    for h in range(H):
                        if h + 1 < H:
                            biased(h + 1, nb)
                        combined(h, nb)
                    step.reset()
                tiles(dve, body)

            @block.scalar
            def _(act):
                step = Steps(act, act_c)

                def exps(h, nb):
                    take(act, T["e_ready"])
                    u = h % 2
                    for m in range(2):
                        step(nc.scalar.activation(e[:, u, m, 0:nb * BANK], e[:, u, m, 0:nb * BANK], ACT.Exp,
                                                  bias=nmx[:, u, m:m + 1], accum_out=z[:, u, m:m + 1]))
                    step.tell(T["p_ready"])

                def turned(h, nb):
                    take(act, T["wT_psum"])
                    act.sem_inc(T["w_free"], 1)
                    step(nc.scalar.copy(wT[:, 0:4 * nb, :].rearrange("p j n -> p (j n)"), flat(psum[:, 4:4 + nb, :])))
                    step.tell(T["wT_ready"], T["wT_free"])

                def body(t, nb):
                    exps(0, nb)
                    for h in range(H):
                        if h + 1 < H:
                            exps(h + 1, nb)
                        turned(h, nb)
                    take(act, T["o_ready"])
                    step(nc.scalar.copy(flat(o_att[:, ds(t, 1), :]), psum[:, 6, :]))
                    step.tell(T["o_free"])
                    step.reset()
                tiles(act, body)


def toeplitz(nc, A, sem, sbuf, psum, toep_dram, strip):
    with ExitStack() as st:
        rel = sbuf(st, "rel_bias", [BUCKETS + 1, H])
        relw = sbuf(st, "rel_wide", [BUCKETS + 1, H, P])
        hot = sbuf(st, "onehot", [BUCKETS + 1, TOEP])
        rows = sbuf(st, "bias_rows", [P, H, TOEP])
        land, out, back, wide, ps, pf, ev = (sem("tp_" + n) for n in "land out back wide psum free rows".split())
        dve_c = sem("tp_dve")
        cuts = [(a, min(BANK, TOEP - a)) for a in range(0, TOEP, BANK)]
        with nc.Block() as block:
            @block.sync
            def _(sp):
                sp.dma_start(rel[0:BUCKETS, :], A["rel_bias"]).then_inc(land, 16)
                sp.dma_start(hot[:], A["const_onehot"]).then_inc(land, 16)
                for h in range(H):
                    sp.wait_ge(ev, h + 1)
                    sp.dma_start(toep_dram[h], rows[:, h, :]).then_inc(out, 16)
                sp.wait_ge(out, 16 * H)
                for h in range(H):
                    f = toep_dram[h].rearrange("q m -> (q m)")[P - 1:P - 1 + P * (TOEP - 1)]
                    sp.dma_start(strip[:, h, :], f.rearrange("(q m) -> q m", q=P)[:, 0:STRIP]).then_inc(back, 16)
                sp.wait_ge(back, 16 * H)

            @block.tensor
            def _(pe):
                pe.wait_ge(wide, 1)
                pe.wait_ge(land, 32)
                for h in range(H):
                    if h >= 2:
                        pe.wait_ge(ev, h - 1)
                    for n, (a, w) in enumerate(cuts):
                        ins = nc.tensor.matmul(psum[:, 4 * (h % 2) + n, 0:w], relw[:, h, :], hot[:, a:a + w], start=True, stop=True)
                    ins.then_inc(ps, 1)

            @block.vector
            def _(dve):
                step = Steps(dve, dve_c)
                step(nc.vector.memset(rel[BUCKETS:BUCKETS + 1, :], MASKED))
                dve.wait_ge(land, 32)
                step.done()
                step(nc.vector.tensor_copy(relw[:], over(rel[:], P)))
                step.tell(wide)

            @block.scalar
            def _(act):
                for h in range(H):
                    act.wait_ge(ps, h + 1)
                    f = psum[:, 4 * (h % 2):4 * (h % 2) + 4, :].rearrange("p b n -> p (b n)")[:, 0:TOEP]
                    nc.scalar.copy(rows[:, h, :], f).then_inc(ev, 1)


def sample_attention(nc, A, sem, sbuf, psum, ident, lam, qT, kT, v, o_att, **_):
    R = H * 2 * NT
    CH = 4
    NCH = PAGES // CH
    WROW = 2 + AW + NB * R
    with ExitStack() as st:
        pt = sbuf(st, "page_table", [1, NB * PAGES], I32)
        kp = sbuf(st, "k_pages", [P, 2, CH, AW])
        vp = sbuf(st, "v_pages", [P, 2, CH, AW])
        kpT = sbuf(st, "k_pagesT", [P, 2, H, CH * P])
        q_all = sbuf(st, "q_rows", [P, NB, H, R])
        q_now = sbuf(st, "q_rows_now", [P, H, R])
        rel = sbuf(st, "rel_bias_s", [BUCKETS + 1, H])
        relr = sbuf(st, "rel_rows", [BUCKETS + 1, NT, H, 2, NT])
        hot = sbuf(st, "onehot_tail", [BUCKETS + 1, NT, TAIL + 1])
        rows = sbuf(st, "row_consts", [R, WROW])
        tail = sbuf(st, "tail_bias", [R, TAIL])
        far = sbuf(st, "far_bias", [R, 1])
        coef = sbuf(st, "map_coef", [R, 1])
        vb = sbuf(st, "v_new", [NT, NB, AW])
        vb_now = sbuf(st, "v_new_now", [NT, AW])
        sc = sbuf(st, "scores_s", [R, PAST + NT])
        pT = sbuf(st, "probsT", [P, PAGES + 1, R])
        mx, nmx, rz = (sbuf(st, n, [R, 1]) for n in ("mx_s", "nmx_s", "rz_s"))
        mxs, z = sbuf(st, "mx_chunks", [R, NCH]), sbuf(st, "z_parts", [R, NCH // 2])
        ex = qT[0:R].rearrange("r h n -> r (h n)")
        comb = sbuf(st, "comb_now", [R, NS])
        om = sbuf(st, "o_masked", [R, AW])
        zero = sbuf(st, "zeros_s", [R, NS + AW])
        T = {n: sem("sa_" + n) for n in
             ("tab small q_ready bias_psum setup k_free0 k_free1 k_land0 k_land1 v_free0 v_free1 v_land0 v_land1 "
              "kT_act kT_dve kT_done_act kT_done_dve kT_free_act kT_free_dve s_ready s_free s_copied q_now max_ready "
              "exp_ready z_ready pT_psum pT_ready pT_free o_psum om_ready om_free sum_ready").split()}
        dve_c, act_c = sem("sa_dve"), sem("sa_act")

        EXPS, VSLOT = NCH // 2, 3

        def exp_cols(p):
            return slice(p * 2 * BANK, (p + 1) * 2 * BANK + (NT if p == EXPS - 1 else 0))

        def samples(eng, body):
            body(0, None)
            with eng.Fori(0, NB - 1) as i:
                body(i + 1, i)
            body(None, NB - 1)

        with nc.Block() as block:
            @block.sync
            def _(sp):
                sp.dma_start(pt[:], A["page_table"].rearrange("(a b) n -> a (b n)", a=1)).then_inc(T["tab"], 16)
                sp.dma_start(rel[0:BUCKETS, :], A["rel_bias"]).then_inc(T["small"], 16)
                sp.dma_start(hot[:], A["const_tail"]).then_inc(T["small"], 16)
                sp.dma_start(rows[:], A["const_rows"]).then_inc(T["small"], 16)
                for b in range(NB):
                    sp.dma_start(vb[:, b, :], v[b * NT:(b + 1) * NT, TILES, :]).then_inc(T["small"], 16)
                sp.wait_ge(T["tab"], 16)
                cache_k = A["cache_k"][0].rearrange("g p h m d -> g p (h m d)")
                cache_v = A["cache_v"][0].rearrange("g p h d -> g p (h d)")

                def load(cache, slots, x, b, c):
                    u = c % 2
                    take(sp, T[f"{x}_free{u}"])
                    pages = [sp.value_load(pt[0:1, ds(b * PAGES + (c * CH + g), 1)], min_val=0, max_val=POOL - 1)
                             for g in range(CH)]
                    for g, page in enumerate(pages):
                        sp.dma_start(slots[:, u, g, :], cache[ds(page, 1)].rearrange("a p n -> (a p) n"))\
                            .then_inc(T[f"{x}_land{u}"], 16)

                def body(b, prev):
                    for c in range(NCH):
                        if b is not None:
                            load(cache_k, kp, "k", b, c)
                        if prev is not None and c >= NCH // 2:
                            for j in range(2):
                                load(cache_v, vp, "v", prev, 2 * (c - NCH // 2) + j)
                samples(sp, body)

            @block.tensor
            def _(pe):
                for x in "kv":
                    for u in range(2):
                        pe.sem_inc(T[f"{x}_free{u}"], 1)
                pe.sem_inc(T["kT_free_act"], 2)
                pe.sem_inc(T["kT_free_dve"], 2)
                pe.sem_inc(T["s_free"], 1)
                pe.sem_inc(T["pT_free"], 1)
                pe.sem_inc(T["om_free"], 1)
                pe.wait_ge(T["q_ready"], 1)
                for t in range(NT):
                    ins = nc.tensor.matmul(psum[0:R, 0, 0:TAIL + 1], relr[:, t].rearrange("p h m t -> p (h m t)"), hot[:, t, :],
                                           start=(t == 0), stop=(t == NT - 1))
                ins.then_inc(T["bias_psum"], 1)
                pe.wait_ge(T["setup"], 1)
                nc.tensor.matmul(psum[0:NS, 6, :], zero[:, 0:NS], zero[:, NS:], start=True, stop=False, skip_group_check=True)

                def turn_keys(c):
                    u = c % 2
                    take(pe, T[f"k_land{u}"], 16 * CH)
                    for h in range(H):
                        who = "act" if h % 2 else "dve"
                        take(pe, T[f"kT_free_{who}"])
                        for g in range(CH):
                            ins = nc.tensor.transpose(psum[:, h, g * P:(g + 1) * P], kp[:, u, g, h * P:(h + 1) * P], ident[:])
                        ins.then_inc(T[f"kT_{who}"], 1)

                def score(c):
                    for h in range(H):
                        take(pe, T["kT_done_act" if h % 2 else "kT_done_dve"])
                        if h == 0:
                            take(pe, T["s_free"])
                        ins = nc.tensor.matmul(psum[0:R, 4, :], q_now[:, h, :], kpT[:, c % 2, h, :],
                                               start=(h == 0), stop=(h == H - 1))
                    ins.then_inc(T["s_ready"], 1)

                def score_new(b):
                    take(pe, T["s_free"])
                    for h in range(H):
                        ins = nc.tensor.matmul(psum[0:R, 4, 0:NT], q_now[:, h, :], kT[:, h, ds(b * NT + SEQ, NT)],
                                               start=(h == 0), stop=(h == H - 1))
                    ins.then_inc(T["s_ready"], 1)

                def turn_probs(g):
                    if g < EXPS:
                        take(pe, T["exp_ready"])
                    take(pe, T["pT_free"])
                    for j in range(8 if g < EXPS else 1):
                        at = (g * 8 + j) * P
                        n = P if g < EXPS else NT
                        col = j * R
                        ins = nc.tensor.transpose(psum[0:n, 5, col:col + R], ex[:, at:at + n], ident[0:R, 0:R])
                    ins.then_inc(T["pT_psum"], 1)

                def values(c):
                    take(pe, T[f"v_land{c % 2}"], 16 * CH)
                    if c % 2 == 0:
                        take(pe, T["pT_ready"])
                    for g in range(CH):
                        ins = nc.tensor.matmul(psum[0:R, 7, :], pT[:, c * CH + g, :], vp[:, c % 2, g, :],
                                               start=(c == 0 and g == 0), stop=False)
                    ins.then_inc(T[f"v_free{c % 2}"], 1)

                def body(b, prev):
                    if b is not None:
                        take(pe, T["q_now"])
                        turn_keys(0)
                    for c in range(NCH):
                        if b is not None:
                            if c + 1 < NCH:
                                turn_keys(c + 1)
                            score(c)
                        if prev is not None:
                            if 1 <= c <= EXPS + 1:
                                turn_probs(c - 1)
                            if VSLOT <= c < VSLOT + NCH // 2:
                                values(2 * (c - VSLOT))
                                values(2 * (c - VSLOT) + 1)
                            if c == VSLOT + NCH // 2 - 1:
                                take(pe, T["pT_ready"])
                                nc.tensor.matmul(psum[0:R, 7, :], pT[0:NT, PAGES, :], vb_now[:],
                                                 start=False, stop=True).then_inc(T["o_psum"], 1)
                    if b is not None:
                        score_new(b)
                    if prev is not None:
                        take(pe, T["om_ready"])
                        nc.tensor.matmul(psum[0:NS, 6, :], comb[:], om[:], start=False, stop=False,
                                         skip_group_check=True).then_inc(T["om_free"], 1)
                samples(pe, body)
                for u in range(2):
                    take(pe, T[f"v_free{u}"])
                    take(pe, T[f"k_free{u}"])

            @block.scalar
            def _(act):
                step = Steps(act, act_c)
                act.wait_ge(T["setup"], 1)

                def copy_keys(c):
                    for h in (1, 3):
                        take(act, T["kT_act"])
                        if h == 3:
                            act.sem_inc(T[f"k_free{c % 2}"], 1)
                        step(nc.scalar.copy(kpT[:, c % 2, h, :], psum[:, h, :]))
                        step.tell(T["kT_done_act"], T["kT_free_act"])

                def body(b, prev):
                    if b is not None:
                        copy_keys(0)
                    for c in range(NCH):
                        if b is not None and c + 1 < NCH:
                            copy_keys(c + 1)
                        if prev is not None and c < EXPS:
                            if c == 0:
                                take(act, T["max_ready"])
                            s = exp_cols(c)
                            step(nc.scalar.activation(ex[:, s], sc[:, s], ACT.Exp, bias=nmx[:], accum_out=z[:, c:c + 1]))
                            step.tell(*([T["exp_ready"]] + ([T["z_ready"]] if c == EXPS - 1 else [])))
                        if b is not None:
                            take(act, T["s_ready"])
                            step(nc.scalar.activation(sc[:, c * BANK:(c + 1) * BANK], psum[0:R, 4, :], ACT.Identity, bias=far[:]))
                            step.tell(T["s_free"], T["s_copied"])
                    if b is not None:
                        take(act, T["s_ready"])
                        step(nc.scalar.activation(sc[:, PAST:PAST + NT], psum[0:R, 4, 0:NT], ACT.Identity, bias=far[:]))
                        step.tell(T["s_free"], T["s_copied"])
                    step.reset()
                samples(act, body)
                act.wait_ge(T["sum_ready"], 1)
                nc.scalar.copy(o_att[0:NS, TILES, :], psum[0:NS, 6, :]).then_inc(act_c, 1)
                act.wait_ge(act_c, 1)

            @block.vector
            def _(dve):
                step = Steps(dve, dve_c)
                step(nc.vector.memset(rel[BUCKETS:BUCKETS + 1, :], MASKED))
                step(nc.vector.memset(relr[:], 0.0))
                step(nc.vector.memset(q_all[:], 0.0))
                step(nc.vector.memset(zero[:], 0.0))
                dve.wait_ge(T["small"], 16 * (3 + NB))
                step.done()
                for t in range(NT):
                    for m in range(2):
                        step(nc.vector.tensor_copy(relr[:, t, :, m, t], rel[:]))
                for h in range(H):
                    for m in range(2):
                        part = slice(m * DH, (m + 1) * DH)
                        r = h * 2 * NT + m * NT
                        step(nc.vector.tensor_copy(q_all[part, :, h, r:r + NT],
                                                   qT[part, h, SEQ:SEQ + NS].rearrange("p (b t) -> p b t", t=NT)))
                step.tell(T["q_ready"])
                dve.wait_ge(T["bias_psum"], 1)
                step(nc.vector.tensor_copy(far[:], psum[0:R, 0, TAIL:TAIL + 1]))
                step.done()
                step(nc.vector.tensor_scalar(tail[:], psum[0:R, 0, 0:TAIL], far[:], None, ALU.subtract))
                step(nc.vector.tensor_scalar(coef[:], rows[:, 1:2], lam[0:R, 1:2], rows[:, 0:1], ALU.mult, ALU.add))
                step.tell(T["setup"], T["setup"])
                step.reset()
                mask, combs = rows[:, 2:2 + AW], rows[:, 2 + AW:].rearrange("p (b n) -> p b n", b=NB)

                def copy_keys(c):
                    for h in (0, 2):
                        take(dve, T["kT_dve"])
                        step(nc.vector.tensor_copy(kpT[:, c % 2, h, :], psum[:, h, :]))
                        step.tell(T["kT_done_dve"], T["kT_free_dve"])

                def body(b, prev):
                    if b is not None:
                        step(nc.vector.tensor_copy(q_now[:], q_all[:, ds(b, 1)].rearrange("p a h r -> p (a h) r")))
                        step.tell(T["q_now"])
                        copy_keys(0)
                    if prev is not None:
                        step(nc.vector.tensor_copy(vb_now[:], vb[:, ds(prev, 1), :].rearrange("p a n -> p (a n)")))
                    for c in range(NCH):
                        if b is not None and c + 1 < NCH:
                            copy_keys(c + 1)
                        if b is not None:
                            take(dve, T["s_copied"])
                            if c < NCH - 1:
                                step(nc.vector.tensor_reduce(mxs[:, c:c + 1], sc[:, c * BANK:(c + 1) * BANK], AX, ALU.max))
                        if prev is not None and 1 <= c <= EXPS + 1:
                            take(dve, T["pT_psum"])
                            g = c - 1
                            if g < EXPS:
                                step(nc.vector.tensor_copy(pT[:, g * 8:(g + 1) * 8, :].rearrange("p g r -> p (g r)"),
                                                           psum[:, 5, 0:8 * R]))
                            else:
                                step(nc.vector.tensor_copy(pT[0:NT, PAGES, :], psum[0:NT, 5, 0:R]))
                            step.tell(T["pT_ready"], T["pT_free"])
                        if prev is not None and c == EXPS + 1:
                            take(dve, T["z_ready"])
                            step(nc.vector.tensor_reduce(rz[:], z[:], AX, ALU.add))
                            step.done()
                            step(nc.vector.reciprocal(rz[:], rz[:]))
                            step.done()
                            step(nc.vector.tensor_tensor(rz[:], rz[:], coef[:], ALU.mult))
                            step.done()
                            take(dve, T["om_free"])
                            step(nc.vector.tensor_scalar(comb[:], combs[:, ds(prev, 1), :].rearrange("p a n -> p (a n)"),
                                                         rz[:], None, ALU.mult))
                    if prev is not None:
                        take(dve, T["o_psum"])
                        step(nc.vector.tensor_tensor(om[:], psum[0:R, 7, :], mask, ALU.mult))
                        step.tell(T["om_ready"])
                    if b is not None:
                        take(dve, T["s_copied"])
                        step(nc.vector.tensor_tensor(sc[:, PAST - P:], sc[:, PAST - P:], tail[:], ALU.add))
                        step.done()
                        step(nc.vector.tensor_reduce(mxs[:, NCH - 1:NCH], sc[:, (NCH - 1) * BANK:], AX, ALU.max))
                        step.done()
                        step(nc.vector.tensor_reduce(mx[:], mxs[:], AX, ALU.max))
                        step.done()
                        step(nc.vector.tensor_scalar(nmx[:], mx[:], -1.0, None, ALU.mult))
                        step.tell(T["max_ready"])
                    step.reset()
                samples(dve, body)
                take(dve, T["om_free"])
                dve.sem_inc(T["sum_ready"], 1)


def bcast_rows(nc, psum, bank, lhsT, row_ap):
    for n in range(2):
        ins = nc.tensor.matmul(psum[:, bank + n, :], lhsT, row_ap[:, n * BANK:(n + 1) * BANK], start=True, stop=True)
    return ins


def mix(nc, A, sem, sbuf, psum, x1_dram, h2_dram, mod_dram, gate2, ident, sel, ones, eps, o_att, o_convT, **_):
    with ExitStack() as st:
        w = sbuf(st, "w_out", [P, KD, D])
        mod = sbuf(st, "mod_rest", [NC, 4 * D])
        gate = sbuf(st, "gate1", [P, 2, D])
        sc2, sh2 = sbuf(st, "scale2", [P, 2, D]), sbuf(st, "shift2", [P, 2, D])
        lnr = sbuf(st, "ln1_rows", [1, 2, D])
        lng = sbuf(st, "ln1", [P, 2, D])
        subr = sbuf(st, "subln_row", [1, DV])
        sub = sbuf(st, "subln", [P, DV])
        x = sbuf(st, "x_res", [P, 2, D])
        o_now = sbuf(st, "o_now", [P, 2, AW])
        c_now = sbuf(st, "oc_now", [P, 2, H, P])
        sq = sbuf(st, "o_sq", [P, 2, AW])
        oT = sbuf(st, "oT", [P, 2, H, P])
        ss, rt = sbuf(st, "ss", [P, H]), sbuf(st, "rt", [P, H])
        t1 = sbuf(st, "t1", [P, D])
        x1 = sbuf(st, "x1_out", [P, 2, D])
        h2 = sbuf(st, "h2_out", [P, 2, D])
        bn, ag, sd = sbuf(st, "bn1", [P, 2, 6]), sbuf(st, "ag1", [P, 2]), sbuf(st, "sd1", [P, 1])
        T = {n: sem("mx_" + n) for n in
             ("w_land small rows_psum rows_free staged o_free x_land0 x_land1 x_free0 x_free1 ss_ready rt_ready on_ready "
              "oT_psum oT_ready mix_psum mix_free var_ready sd_ready rows_ready x1_ready0 x1_ready1 stored0 stored1").split()}
        TURN = (0, 5)
        dve_c, act_c, pool_c = sem("mx_dve"), sem("mx_act"), sem("mx_pool")
        x_t = A["x_prompt"][0].rearrange("(t p) d -> p t d", p=P)
        x1_t = x1_dram[0:SEQ, :].rearrange("(t p) d -> p t d", p=P)
        h2_t = h2_dram[0:SEQ, :].rearrange("(t p) d -> p t d", p=P)
        ROWS = [(sel[:, s], mod[:, (kind - GATE1) * D:(kind - GATE1 + 1) * D], dst[:, s])
                for kind, dst in ((GATE1, gate), (SCALE2, sc2), (SHIFT2, sh2), (GATE2, gate2)) for s in range(2)]
        ROWS += [(ones[0:1, :], lnr[:, j, :], lng[:, j]) for j in range(2)]

        def tiles(eng, ahead, rest, rest_first=False):
            def both(u, t, after):
                if rest_first:
                    rest(u, t)
                ahead(1 - u, after)
                if not rest_first:
                    rest(u, t)

            ahead(0, 0)
            with eng.Fori(0, TILES // 2 - 1) as i:
                for u in range(2):
                    both(u, i * 2 + u, i * 2 + (u + 1))
            for t in (TILES - 2, TILES - 1):
                both(t % 2, t, t + 1 if t + 1 < TILES else None)
            rest(0, None)

        def nothing(u, t):
            pass

        with nc.Block() as block:
            @block.sync
            def _(sp):
                sp.dma_start(lnr[:, 0, :], A["ln1_g"]).then_inc(T["small"], 16)
                sp.dma_start(lnr[:, 1, :], A["ln1_b"]).then_inc(T["small"], 16)
                sp.dma_start(subr[:], A["subln_w"]).then_inc(T["small"], 16)
                sp.dma_start(mod[:], mod_dram[:, GATE1 * D:]).then_inc(T["small"], 16)
                sp.dma_start(w[:], A["w_out"][0].rearrange("(k p) n -> p k n", p=P)).then_inc(T["w_land"], 16)

                def body(u, t):
                    take(sp, T[f"x_free{u}"])
                    if t is None:
                        sp.dma_start(x[0:NS, u, :], A["x_sample"].rearrange("b t d -> (b t) d")).then_inc(T[f"x_land{u}"], 16)
                    else:
                        sp.dma_start(x[:, u, :], flat(x_t[:, ds(t, 1), :])).then_inc(T[f"x_land{u}"], 16)
                tiles(sp, nothing, body)

            @block.gpsimd
            def _(pool):
                step = Steps(pool, pool_c)

                def body(u, t):
                    take(pool, T["o_free"])
                    if t is None:
                        step(nc.gpsimd.tensor_copy(o_now[0:NS, u, :], o_att[0:NS, TILES, :]))
                        step(nc.gpsimd.tensor_copy(c_now[:, u, :, 0:NS], o_convT[:, :, SEQ:SEQ + NS]))
                    else:
                        step(nc.gpsimd.tensor_copy(o_now[:, u, :], flat(o_att[:, ds(t, 1), :])))
                        step(nc.gpsimd.tensor_copy(c_now[:, u], o_convT[:, :, ds(t * P, P)]))
                    step.tell(T["staged"])
                    step.reset()
                tiles(pool, body, nothing)

            @block.tensor
            def _(pe):
                pe.sem_inc(T["o_free"], 2)
                pe.sem_inc(T["x_free0"], 1)
                pe.sem_inc(T["x_free1"], 1)
                pe.wait_ge(T["small"], 64)
                for n, (lhsT, row, _) in enumerate(ROWS):
                    if n >= 2:
                        take(pe, T["rows_free"])
                    bcast_rows(nc, psum, 4 + 2 * (n % 2), lhsT, row).then_inc(T["rows_psum"], 1)
                take(pe, T["rows_free"])
                nc.tensor.matmul(psum[:, 4, 0:DV], ones[0:1, :], subr[:], start=True, stop=True).then_inc(T["rows_psum"], 1)
                pe.wait_ge(T["w_land"], 16)

                def turn(u, t):
                    n = NS if t is None else P
                    take(pe, T["on_ready"])
                    for h in range(H):
                        ins = nc.tensor.transpose(psum[:, TURN[u], h * P:h * P + n], sq[0:n, u, h * P:(h + 1) * P], ident[0:n, 0:n])
                    ins.then_inc(T["oT_psum"], 1)

                def product(u, t):
                    n = NS if t is None else P
                    take(pe, T["mix_free"])
                    take(pe, T["oT_ready"])
                    for k in range(KD):
                        lhsT = oT[:, u, k, 0:n] if k < H else c_now[:, u, k - H, 0:n]
                        for c in range(2):
                            ins = nc.tensor.matmul(psum[0:n, 1 + 2 * u + c, :], lhsT, w[:, k, c * BANK:(c + 1) * BANK],
                                                   start=(k == 0), stop=(k == KD - 1))
                    ins.then_inc(T["mix_psum"], 1)
                tiles(pe, turn, product, rest_first=True)

            @block.scalar
            def _(act):
                step = Steps(act, act_c)
                for n in range(len(ROWS) + 1):
                    take(act, T["rows_psum"])
                    if n < len(ROWS):
                        step(nc.scalar.copy(ROWS[n][2], flat(psum[:, 4 + 2 * (n % 2):6 + 2 * (n % 2), :])))
                    else:
                        step(nc.scalar.mul(sub[:], psum[:, 4, 0:DV], 1.0 - LAM_INIT))
                    step.tell(T["rows_free"])
                step.tell(T["rows_ready"])
                act.sem_inc(T["stored0"], 32)
                act.sem_inc(T["stored1"], 32)
                step.reset()

                def ahead(u, t):
                    n = NS if t is None else P
                    take(act, T["ss_ready"])
                    step(nc.scalar.activation(rt[0:n, :], ss[0:n, :], ACT.Sqrt, bias=eps[0:n, :], scale=1.0 / DV))
                    step.tell(T["rt_ready"])
                    take(act, T["oT_psum"])
                    step(nc.scalar.copy(oT[:, u, :, 0:n], psum[:, TURN[u], :].rearrange("p (h n) -> p h n", h=H)[:, :, 0:n]))
                    step.tell(T["oT_ready"])
                    step.reset()

                def rest(u, t):
                    n = NS if t is None else P
                    take(act, T["var_ready"])
                    step(nc.scalar.activation(sd[0:n, :], ag[0:n, 1:2], ACT.Sqrt, bias=eps[0:n, :]))
                    step.tell(T["sd_ready"])
                    take(act, T[f"x1_ready{u}"])
                    if t is None:
                        for g in range(P // NS):
                            rows = slice(SEQ + g * NS, SEQ + (g + 1) * NS)
                            act.dma_start(x1_dram[rows, :], x1[0:NS, u, :]).then_inc(T[f"stored{u}"], 16)
                            act.dma_start(h2_dram[rows, :], h2[0:NS, u, :]).then_inc(T[f"stored{u}"], 16)
                    else:
                        act.dma_start(flat(x1_t[:, ds(t, 1), :]), x1[:, u, :]).then_inc(T[f"stored{u}"], 16)
                        act.dma_start(flat(h2_t[:, ds(t, 1), :]), h2[:, u, :]).then_inc(T[f"stored{u}"], 16)
                    step.reset()
                tiles(act, ahead, rest)
                act.wait_ge(T["stored0"], 32 * (P // NS))
                act.wait_ge(T["stored1"], 32)

            @block.vector
            def _(dve):
                step = Steps(dve, dve_c)
                dve.sem_inc(T["mix_free"], 2)
                dve.wait_ge(T["rows_ready"], 1)
                step(nc.vector.tensor_scalar(sc2[:], sc2[:], 1.0, None, ALU.add))
                step.reset()

                def ahead(u, t):
                    n = NS if t is None else P
                    take(dve, T["staged"])
                    for h in range(H):
                        o = o_now[0:n, u, h * DV:(h + 1) * DV]
                        step(nc.vector.tensor_tensor_reduce(sq[0:n, u, h * DV:(h + 1) * DV], o, o, 1.0, 0.0, ALU.mult, ALU.add,
                                                            ss[0:n, h:h + 1]))
                    step.tell(T["ss_ready"])
                    take(dve, T["rt_ready"])
                    step(nc.vector.reciprocal(rt[0:n, :], rt[0:n, :]))
                    step.done()
                    for h in range(H):
                        s = slice(h * DV, (h + 1) * DV)
                        step(nc.vector.scalar_tensor_tensor(out=sq[0:n, u, s], in0=o_now[0:n, u, s], scalar=rt[0:n, h:h + 1],
                                                            in1=sub[0:n, :], op0=ALU.mult, op1=ALU.mult))
                    step.tell(T["on_ready"])
                    step.reset()

                def rest(u, t):
                    n = NS if t is None else P
                    take(dve, T["mix_psum"])
                    dve.sem_inc(T["o_free"], 1)
                    step(nc.vector.tensor_tensor(t1[0:n, :], flat(psum[0:n, 1 + 2 * u:3 + 2 * u, :]), gate[0:n, int(t is None), :], ALU.mult))
                    step.tell(T["mix_free"])
                    take(dve, T[f"x_land{u}"], 16)
                    step(nc.vector.scalar_tensor_tensor(out=t1[0:n, :], in0=x[0:n, u, :], scalar=ALPHA, in1=t1[0:n, :],
                                                        op0=ALU.mult, op1=ALU.add))
                    step.tell(T[f"x_free{u}"])
                    for c in range(2):
                        step(nc.vector.bn_stats(bn[0:n, c, :], t1[0:n, c * BANK:(c + 1) * BANK]))
                    step.done()
                    step(nc.vector.bn_aggr(ag[0:n, :], bn[0:n].rearrange("p a b -> p (a b)")))
                    step.tell(T["var_ready"])
                    take(dve, T["sd_ready"])
                    step(nc.vector.reciprocal(sd[0:n, :], sd[0:n, :]))
                    step.done()
                    step(nc.vector.tensor_scalar(t1[0:n, :], t1[0:n, :], ag[0:n, 0:1], sd[0:n, :], ALU.subtract, ALU.mult))
                    step.done()
                    step(nc.vector.tensor_tensor(t1[0:n, :], t1[0:n, :], lng[0:n, 0, :], ALU.mult))
                    step.done()
                    take(dve, T[f"stored{u}"], 32)
                    step(nc.vector.tensor_tensor(x1[0:n, u, :], t1[0:n, :], lng[0:n, 1, :], ALU.add))
                    step.done()
                    s = int(t is None)
                    step(nc.vector.tensor_tensor(h2[0:n, u, :], x1[0:n, u, :], sc2[0:n, s, :], ALU.mult))
                    step.done()
                    step(nc.vector.tensor_tensor(h2[0:n, u, :], h2[0:n, u, :], sh2[0:n, s, :], ALU.add))
                    step.tell(T[f"x1_ready{u}"])
                    step.reset()
                tiles(dve, ahead, rest)


def peer(nc, A, sem, sbuf, psum, x1_dram, h2_dram, ident, ones, eps, gate2, **_):
    GROUPS = SEL // GROUP
    COPIES = P // NS
    USES = SEL // RING
    with ExitStack() as st:
        w = sbuf(st, "w_pq", [P, KD, HP * P])
        subT = sbuf(st, "sub_keysT", [P, HP, PK])
        ring = sbuf(st, "ring", [P, RING, 2 * D])
        stage = sbuf(st, "index_stage", [P, 4, GROUP], U32)
        e_all = sbuf(st, "experts", [P, TILES + 1, SEL], U32)
        g_all = sbuf(st, "gates", [P, TILES + 1, SEL])
        h_sel = sbuf(st, "h2_next", [P, D])
        h_cur = sbuf(st, "h2_now", [P, D])
        hT = sbuf(st, "h2T", [P, KD, P])
        sc = sbuf(st, "scores_pk", [P, HP, PK])
        qT = sbuf(st, "queriesT", [P, HP, P])
        x_res = sbuf(st, "x1_res", [P, D])
        f = sbuf(st, "f", [P, D])
        lng = sbuf(st, "ln2", [P, 2, D])
        fold = sbuf(st, "fold", [P, P])
        diag = sbuf(st, "diag", [P, 2, GROUP, P])
        dots, act_g, wgt = (sbuf(st, n, [P, 2, GROUP]) for n in ("dots", "gelu", "expert_w"))
        sv, si, sif = sbuf(st, "sv", [P, 2, TOPK]), sbuf(st, "si", [P, 2, TOPK], U32), sbuf(st, "sif", [P, 2, TOPK])
        cand, iota, hot = sbuf(st, "cand", [P, TOPK, TOPK]), sbuf(st, "iota16", [P, TOPK]), sbuf(st, "hot", [P, TOPK, TOPK])
        cv = sbuf(st, "cv", [P, PH, TOPK])
        ci, cab, cabf = sbuf(st, "ci", [P, TOPK], U32), sbuf(st, "cab", [P, 2, TOPK], U32), sbuf(st, "cabf", [P, 2, TOPK])
        eab = sbuf(st, "eab", [P, 2, PH, TOPK])
        gsum = sbuf(st, "gsum", [P, PH])
        bn, ag, sd = sbuf(st, "bn2", [P, 2, 6]), sbuf(st, "ag2", [P, 2]), sbuf(st, "sd2", [P, 1])
        T = {n: sem("pr_" + n) for n in
             ("w_land consts rows_psum rows_free rows_ready sub_psum sub_free setup_pe "
              "hsel_land hsel_free_pe hsel_free_act hsel_now hT_psum hT_ready qp_psum qp_ready qT_psum qT_ready sc_psum sc_ready sc_free "
              "e_ready staged hcur_ready hcur_free dots_ready dots_free diag_ready diag_free f_psum f_free f_ready "
              "gx_ready gx_done g_ready var_ready sd_ready y_ready y_stored xres_land xres_free w_free").split()}
        land = [sem(f"pr_land{s}") for s in range(RING)]
        slot_free = [sem(f"pr_slot_free{s}") for s in range(RING)]
        dve_c, act_c, pool_c = sem("pr_dve"), sem("pr_act"), sem("pr_pool")
        h2_t = h2_dram.rearrange("(t p) d -> p t d", p=P)
        x1_t = x1_dram.rearrange("(t p) d -> p t d", p=P)
        y_t = A["y_prompt"][0].rearrange("(t p) d -> p t d", p=P)
        uv = A["uv"]

        def run(eng, expert, select, finish=lambda t, c: None, tidy=lambda: None):
            def beside(t, before, after):
                for c in range(GROUPS):
                    expert(t, c)
                    if not isinstance(before, str):
                        finish(before, c)
                    if not isinstance(after, str):
                        select(after, c)
                tidy()

            for c in range(GROUPS):
                select(0, c)
            beside(0, "none", 1)
            with eng.Fori(1, TILES - 1) as t:
                beside(t, t - 1, t + 1)
            beside(TILES - 1, TILES - 2, None)
            beside(None, TILES - 1, "none")
            for c in range(GROUPS):
                finish(None, c)
            tidy()

        def index(t):
            return TILES if t is None else t

        def groups_of(t):
            return GROUPS // COPIES if t is None else GROUPS

        with nc.Block() as block:
            @block.sync
            def _(sp):
                sp.dma_start(w[:], A["w_pq"][0].rearrange("(k p) n -> p k n", p=P)).then_inc(T["w_land"], 16)
                sp.dma_start(qT[:], A["sub_keys"][0].rearrange("h q n d -> n (h q) d")).then_inc(T["consts"], 16)
                sp.dma_start(f[0:1, :], A["ln2_g"]).then_inc(T["consts"], 16)
                sp.dma_start(h_cur[0:1, :], A["ln2_b"]).then_inc(T["consts"], 16)
                sp.dma_start(fold[:], A["const_fold"]).then_inc(T["consts"], 16)
                sp.dma_start(iota[:], A["const_iota"]).then_inc(T["consts"], 16)

                def select(t, c):
                    if c == 0:
                        take(sp, T["hsel_free_pe"])
                        take(sp, T["hsel_free_act"])
                        sp.dma_start(h_sel[:], flat(h2_t[:, ds(index(t), 1), :])).then_inc(T["hsel_land"], 16)

                def store(t):
                    take(sp, T["y_ready"])
                    if t is None:
                        sp.dma_start(A["y_sample"].rearrange("b t d -> (b t) d"), f[0:NS, :]).then_inc(T["y_stored"], 16)
                    else:
                        sp.dma_start(flat(y_t[:, ds(t, 1), :]), f[:]).then_inc(T["y_stored"], 16)

                def residual(t):
                    take(sp, T["xres_free"])
                    sp.dma_start(x_res[:], flat(x1_t[:, ds(index(t), 1), :])).then_inc(T["xres_land"], 16)

                select(0, 0)
                select(1, 0)
                residual(0)
                with sp.Fori(0, TILES - 2) as i:
                    select(i + 2, 0)
                    store(i)
                    residual(i + 1)
                select(None, 0)
                store(TILES - 2)
                residual(TILES - 1)
                store(TILES - 1)
                residual(None)
                store(None)
                sp.wait_ge(T["y_stored"], 16)

            @block.gpsimd
            def _(pool):
                step = Steps(pool, pool_c)

                def expert(t, c):
                    if c >= groups_of(t):
                        return
                    if c == 0:
                        take(pool, T["e_ready"])
                    for s in range(GROUP):
                        take(pool, slot_free[(c * GROUP + s) % RING])
                        if s == 0:
                            src = e_all[:, ds(index(t), 1), c * GROUP:(c + 1) * GROUP]
                            step(nc.gpsimd.tensor_copy(stage[:, c % 4, :], flat(src)))
                            step.done()
                        slot = (c * GROUP + s) % RING
                        pool.indirect_dma_start(ring[:, slot, :], None, uv,
                                                bass.IndirectOffsetOnAxis(ap=stage[:, c % 4, s:s + 1], axis=0))\
                            .then_inc(land[slot], 16)
                run(pool, expert, lambda t, c: None, tidy=step.reset)

            @block.tensor
            def _(pe):
                for s in range(RING):
                    pe.sem_inc(slot_free[s], 1)
                pe.sem_inc(T["hsel_free_pe"], 1)
                pe.sem_inc(T["diag_free"], 1)
                pe.sem_inc(T["f_free"], 1)
                pe.wait_ge(T["consts"], 5 * 16)
                bcast_rows(nc, psum, 0, ones[0:1, :], f[0:1, :])
                bcast_rows(nc, psum, 2, ones[0:1, :], h_cur[0:1, :])
                for j in range(HP):
                    ins = nc.tensor.transpose(psum[:, 4 + j // 4, (j % 4) * PK:(j % 4 + 1) * PK], qT[:, j, :], ident[:])
                ins.then_inc(T["rows_psum"], 1)
                pe.wait_ge(T["rows_ready"], 1)
                pe.wait_ge(T["w_land"], 16)

                def expert(t, c):
                    last = groups_of(t) - 1
                    if c > last:
                        return
                    if c == 0:
                        take(pe, T["f_free"])
                    for s in range(GROUP):
                        take(pe, T["diag_ready"])
                        slot = (c * GROUP + s) % RING
                        for n in range(2):
                            ins = nc.tensor.matmul(psum[:, n, :], diag[:, c % 2, s, :], ring[:, slot, D + n * BANK:D + (n + 1) * BANK],
                                                   start=(c == 0 and s == 0), stop=(c == last and s == GROUP - 1),
                                                   skip_group_check=True)
                            if n == 0 and s == 0:
                                ins.then_inc(T["diag_free"], 1)
                        ins.then_inc(T["f_psum"] if c == last and s == GROUP - 1 else slot_free[slot], 1)

                def select(t, c):
                    if c == 0:
                        take(pe, T["hsel_land"], 16)
                        for k in range(KD):
                            ins = nc.tensor.transpose(psum[:, 2 + k // 4, (k % 4) * P:(k % 4 + 1) * P], h_sel[:, k * P:(k + 1) * P], ident[:])
                        ins.then_inc(T["hT_psum"], 1)
                    elif c <= 8:
                        n, half = (c - 1) // 2, (c - 1) % 2
                        if c == 1:
                            take(pe, T["hT_ready"])
                        for k in range(4 * half, 4 * half + 4):
                            ins = nc.tensor.matmul(psum[:, 4 + n, :], hT[:, k, :], w[:, k, n * BANK:(n + 1) * BANK],
                                                   start=(k == 0), stop=(k == KD - 1), skip_group_check=True)
                        if half:
                            ins.then_inc(T["qp_psum"], 1)
                    elif c in (9, 10):
                        if c == 9:
                            for n in range(4):
                                take(pe, T["qp_ready"])
                        else:
                            take(pe, T["qT_ready"])
                        for j in range(8):
                            hp = (c - 9) * 8 + j
                            ins = nc.tensor.transpose(psum[:, 2 + j // 4, (j % 4) * P:(j % 4 + 1) * P], sc[:, hp, :], ident[:])
                        ins.then_inc(T["qT_psum"], 1)
                    elif c == 11:
                        take(pe, T["qT_ready"])
                        for j in range(HP):
                            ins = nc.tensor.matmul(psum[:, 4 + j // 4, (j % 4) * PK:(j % 4 + 1) * PK], qT[:, j, :], subT[:, j, :],
                                                   start=True, stop=True)
                        ins.then_inc(T["sc_psum"], 1)
                run(pe, expert, select)

            @block.scalar
            def _(act):
                step = Steps(act, act_c)
                act.wait_ge(T["rows_psum"], 1)
                step(nc.scalar.copy(lng[:, 0], flat(psum[:, 0:2, :])))
                step(nc.scalar.copy(lng[:, 1], flat(psum[:, 2:4, :])))
                step(nc.scalar.copy(subT[:].rearrange("p j n -> p (j n)"), flat(psum[:, 4:8, :])))
                step.tell(T["rows_ready"], T["hsel_free_act"])
                step.reset()

                def expert(t, c):
                    last = groups_of(t) - 1
                    if c > last:
                        return
                    if c == 0:
                        take(act, T["hcur_free"])
                        take(act, T["g_ready"])
                        step(nc.scalar.copy(h_cur[:], h_sel[:]))
                        step.tell(T["hcur_ready"], T["hsel_free_act"])
                    u = c % 2
                    take(act, T["dots_ready"])
                    step(nc.scalar.activation(act_g[:, u, :], dots[:, u, :], ACT.Gelu))
                    step.tell(T["dots_free"])
                    for s in range(GROUP):
                        k = c * GROUP + s
                        step(nc.scalar.activation(wgt[:, u, s:s + 1], act_g[:, u, s:s + 1], ACT.Copy,
                                                  scale=g_all[:, ds(index(t), 1), k:k + 1].rearrange("p a b -> p (a b)")))
                    step.done()
                    take(act, T["diag_free"])
                    for s in range(GROUP):
                        nc.scalar.activation(diag[:, u, s, :], (fold if t is None else ident)[:], ACT.Copy,
                                             scale=wgt[:, u, s:s + 1]).then_inc(T["diag_ready"], 1)
                    if c == last:
                        take(act, T["f_psum"])
                        act.sem_inc(slot_free[RING - 1], 1)
                        take(act, T["y_stored"], 16)
                        step(nc.scalar.copy(f[:], flat(psum[:, 0:2, :])))
                        step.tell(T["f_ready"], T["f_free"])

                def select(t, c):
                    if c == 0:
                        take(act, T["hT_psum"])
                        act.sem_inc(T["hsel_free_pe"], 1)
                        step(nc.scalar.copy(hT[:].rearrange("p k n -> p (k n)"), flat(psum[:, 2:4, :])))
                        step.tell(T["hT_ready"])
                    elif c in (2, 4, 6, 8):
                        n = c // 2 - 1
                        if n == 0:
                            take(act, T["sc_free"])
                        take(act, T["qp_psum"])
                        step(nc.scalar.copy(sc[:, 4 * n:4 * n + 4, :].rearrange("p j n -> p (j n)"), psum[:, 4 + n, :]))
                        step.tell(T["qp_ready"])
                    elif c in (9, 10):
                        take(act, T["qT_psum"])
                        j = (c - 9) * 8
                        step(nc.scalar.copy(qT[:, j:j + 8, :].rearrange("p j n -> p (j n)"), flat(psum[:, 2:4, :])))
                        step.tell(T["qT_ready"])
                    elif c == 11:
                        take(act, T["sc_psum"])
                        step(nc.scalar.copy(sc[:].rearrange("p j n -> p (j n)"), flat(psum[:, 4:8, :])))
                        step.tell(T["sc_ready"])
                    elif c == 28:
                        take(act, T["gx_ready"])
                        step(nc.scalar.activation(cv[:], cv[:], ACT.Exp))
                        step.tell(T["gx_done"])

                def finish(t, c):
                    if c == 3:
                        take(act, T["var_ready"])
                        step(nc.scalar.activation(sd[:], ag[:, 1:2], ACT.Sqrt, bias=eps[:]))
                        step.tell(T["sd_ready"])

                act.sem_inc(T["y_stored"], 16)
                run(act, expert, select, finish, step.reset)

            @block.vector
            def _(dve):
                step = Steps(dve, dve_c)
                dve.wait_ge(T["rows_ready"], 1)
                for n in ("hcur_free", "dots_free", "dots_free", "xres_free", "sc_free"):
                    dve.sem_inc(T[n], 1)

                def expert(t, c):
                    last = groups_of(t) - 1
                    if c > last:
                        return
                    if c == 0:
                        take(dve, T["hcur_ready"])
                    take(dve, T["dots_free"])
                    for s in range(GROUP):
                        k = c * GROUP + s
                        slot = k % RING
                        dve.wait_ge(land[slot], (index(t) * USES + (k // RING + 1)) * 16)
                        step(nc.vector.tensor_tensor_reduce(ring[:, slot, 0:D], ring[:, slot, 0:D], h_cur[:], 1.0, 0.0,
                                                            ALU.mult, ALU.add, dots[:, c % 2, s:s + 1]))
                    step.tell(T["dots_ready"])
                    if c == last:
                        dve.sem_inc(T["hcur_free"], 1)

                def best16(values, out, where):
                    for r in range(2):
                        o = slice(8 * r, 8 * r + 8)
                        for v, a, b in zip(values, out, where):
                            step(nc.vector.max(a[:, o], v))
                        step.done()
                        for v, a, b in zip(values, out, where):
                            step(nc.vector.max_index(b[:, o], a[:, o], v))
                        if r == 0:
                            step.done()
                            for v, a, b in zip(values, out, where):
                                step(nc.vector.match_replace(v, a[:, o], v, -3e38))
                        step.done()

                def select(t, c):
                    if 12 <= c < 28:
                        h = (c - 12) // 2
                        if c == 12:
                            take(dve, T["sc_ready"])
                        if c % 2 == 0:
                            best16([sc[:, 2 * h + p, :] for p in range(2)], [sv[:, p] for p in range(2)], [si[:, p] for p in range(2)])
                            step(nc.vector.tensor_copy(sif[:], si[:]))
                            step(nc.vector.tensor_tensor(cand[:], over(sv[:, 0], TOPK),
                                                         sv[:, 1].unsqueeze(1).to_broadcast([P, TOPK, TOPK]), ALU.add))
                            step.done()
                            return
                        best16([cand[:].rearrange("p a b -> p (a b)")], [cv[:, h]], [ci])
                        step(nc.vector.tensor_scalar(cab[:, 0], ci[:], 4, None, ALU.logical_shift_right))
                        step(nc.vector.tensor_scalar(cab[:, 1], ci[:], TOPK - 1, None, ALU.bitwise_and))
                        step.done()
                        step(nc.vector.tensor_copy(cabf[:], cab[:]))
                        for p in range(2):
                            step.done()
                            step(nc.vector.tensor_tensor(hot[:], iota[:].unsqueeze(1).to_broadcast([P, TOPK, TOPK]), over(cabf[:, p], TOPK), ALU.is_equal))
                            step.done()
                            step(nc.vector.tensor_tensor(hot[:], hot[:], sif[:, p].unsqueeze(1).to_broadcast([P, TOPK, TOPK]), ALU.mult))
                            step.done()
                            step(nc.vector.tensor_reduce(eab[:, p, h], hot[:], AX, ALU.add))
                        step.done()
                        if c == 27:
                            dve.sem_inc(T["sc_free"], 1)
                    elif c == 28:
                        ef = [eab[:, p].rearrange("p h k -> p (h k)") for p in range(2)]
                        if t is None:
                            for g in range(COPIES):
                                q, k = slice(g * NS, (g + 1) * NS), slice(g * NS, (g + 1) * NS)
                                step(nc.vector.scalar_tensor_tensor(out=e_all[q, TILES, 0:NS], in0=ef[0][q, k], scalar=float(PK),
                                                                    in1=ef[1][q, k], op0=ALU.mult, op1=ALU.add))
                        else:
                            step(nc.vector.scalar_tensor_tensor(out=flat(e_all[:, ds(t, 1), :]), in0=ef[0], scalar=float(PK), in1=ef[1],
                                                                op0=ALU.mult, op1=ALU.add))
                        less = hot[:, 0:PH, :]
                        step(nc.vector.tensor_tensor(less, cv[:], cv[:, :, 0:1].to_broadcast([P, PH, TOPK]), ALU.subtract))
                        step.done()
                        step(nc.vector.tensor_copy(cv[:], less))
                        step.tell(T["e_ready"], T["gx_ready"])
                    elif c == 29:
                        take(dve, T["gx_done"])
                        step(nc.vector.tensor_reduce(gsum[:], cv[:], AX, ALU.add))
                        step.done()
                        step(nc.vector.reciprocal(gsum[:], gsum[:]))
                        step.done()
                        if t is None:
                            step(nc.vector.tensor_tensor(cv[:], cv[:], over(gsum[:], TOPK), ALU.mult))
                            step.done()
                            gf = cv[:].rearrange("p h k -> p (h k)")
                            for g in range(COPIES):
                                q = slice(g * NS, (g + 1) * NS)
                                step(nc.vector.tensor_copy(g_all[q, TILES, 0:NS], gf[q, q]))
                        else:
                            dst = flat(g_all[:, ds(t, 1), :]).rearrange("p (h k) -> p h k", h=PH)
                            step(nc.vector.tensor_tensor(dst, cv[:], over(gsum[:], TOPK), ALU.mult))
                        step.tell(T["g_ready"])

                def finish(t, c):
                    if c == 2:
                        take(dve, T["f_ready"])
                        step(nc.vector.tensor_tensor(f[:], f[:], gate2[:, int(t is None)], ALU.mult))
                        take(dve, T["xres_land"], 16)
                        step.done()
                        step(nc.vector.scalar_tensor_tensor(out=f[:], in0=x_res[:], scalar=ALPHA, in1=f[:], op0=ALU.mult, op1=ALU.add))
                        step.tell(T["xres_free"])
                        for b in range(2):
                            step(nc.vector.bn_stats(bn[:, b, :], f[:, b * BANK:(b + 1) * BANK]))
                        step.done()
                        step(nc.vector.bn_aggr(ag[:], bn[:].rearrange("p a b -> p (a b)")))
                        step.tell(T["var_ready"])
                    elif c == 4:
                        take(dve, T["sd_ready"])
                        step(nc.vector.reciprocal(sd[:], sd[:]))
                        step.done()
                        step(nc.vector.tensor_scalar(f[:], f[:], ag[:, 0:1], sd[:], ALU.subtract, ALU.mult))
                        step.done()
                        step(nc.vector.tensor_tensor(f[:], f[:], lng[:, 0], ALU.mult))
                        step.done()
                        step(nc.vector.tensor_tensor(f[:], f[:], lng[:, 1], ALU.add))
                        step.tell(T["y_ready"])

                run(dve, expert, select, finish, step.reset)


_INS = ['x_prompt', 'x_sample', 'cache_k', 'cache_v', 'state_conv', 'page_table', 'c_prompt', 'c_sample', 'rel_bias',
        'w_ada', 'b_ada', 'w_in', 'lambda_q1', 'lambda_k1', 'lambda_q2', 'lambda_k2', 'subln_w', 'conv_w', 'w_out',
        'ln1_g', 'ln1_b', 'w_pq', 'sub_keys', 'ln2_g', 'ln2_b']
_OUTS = {'y_prompt': (1, SEQ, D), 'y_sample': (NB, NT, D), 'new_k_prompt': (1, 1, SEQ, H, 2, DH),
         'new_v_prompt': (1, 1, SEQ, H, DV), 'new_conv_prompt': (1, 1, 2, AW), 'new_k_sample': (1, NB, NT, H, 2, DH),
         'new_v_sample': (1, NB, NT, H, DV), 'new_conv_sample': (1, NB, 2, AW)}


def shape_constants():
    def hot(dist):
        n = np.maximum(dist, 0)
        exact = BUCKETS // 2
        large = exact + (np.log(np.maximum(n, exact).astype(np.float32) / np.float32(exact)) / np.float32(math.log(MAX_DIST / exact))
                         * np.float32(BUCKETS - exact)).astype(np.int32)
        bucket = np.where(n < exact, n, np.minimum(large, BUCKETS - 1))
        bucket = np.where(dist < 0, BUCKETS, bucket)
        return (np.arange(BUCKETS + 1)[(slice(None),) + (None,) * dist.ndim] == bucket).astype(np.float32)

    onehot = hot(SEQ + P - 1 - np.arange(TOEP))
    tail = hot(P + np.arange(NT)[:, None] - np.arange(TAIL)[None, :])
    far = hot(np.full((NT, 1), PAST))
    R = H * 2 * NT
    r = np.arange(R)
    head, second, token = r // (2 * NT), (r // NT) % 2, r % NT
    mask = (head[:, None] == np.arange(AW)[None, :] // DV)
    comb = token[:, None, None] + NT * np.arange(NB)[None, :, None] == np.arange(NS)[None, None, :]
    rows = np.concatenate([(second == 0)[:, None], (second == 1)[:, None], mask, comb.reshape(R, NB * NS)], 1).astype(np.float32)
    p = np.arange(P)
    sel = np.zeros((NC, 2, P), np.float32)
    sel[0, 0] = 1
    sel[1 + p % NS // NT, 1, p] = 1
    return {
        'const_ident': np.eye(P, dtype=np.float32),
        'const_fold': (p[:, None] % NS == p[None, :] % NS).astype(np.float32),
        'const_sel': sel,
        'const_onehot': onehot,
        'const_tail': np.concatenate([tail, far], 2).astype(np.float32),
        'const_rows': rows,
        'const_iota': np.broadcast_to(np.arange(TOPK, dtype=np.float32), (P, TOPK)).copy(),
    }


def kernel(**inputs):
    import numpy as _np
    import concourse.bacc as _bacc
    from concourse import mybir as _mybir
    from concourse.bass_utils import run_bass_kernel_spmd as _run

    nc = _bacc.Bacc("TRN2", target_bir_lowering=False, num_devices=1)
    arrays = {name: _np.ascontiguousarray(inputs[name]) for name in _INS}
    arrays['uv'] = _np.concatenate([_np.asarray(inputs['peer_u'])[0], _np.asarray(inputs['peer_v'])[0]], axis=1)
    arrays |= shape_constants()
    A = {}
    for name, a in arrays.items():
        A[name] = nc.dram_tensor(f"in_{name}", a.shape, _mybir.dt.from_np(a.dtype), kind="ExternalInput").ap()
    for name, shape in _OUTS.items():
        A[name] = nc.dram_tensor(f"out_{name}", shape, _mybir.dt.float32, kind="ExternalOutput").ap()
    build(nc, A)
    r = _run(nc, [{f"in_{name}": a for name, a in arrays.items()}], core_ids=[0])
    return tuple(r.results[0][f"out_{name}"] for name in _OUTS)
```

```python
import math
from contextlib import ExitStack

import numpy as np

import concourse.bass as bass
from concourse import mybir

F32 = mybir.dt.float32
U32 = mybir.dt.uint32
I32 = mybir.dt.int32
ALU = mybir.AluOpType
ACT = mybir.ActivationFunctionType
AX = mybir.AxisListType.X
ds = bass.ds

P = 128
D = 1024
KD = D // P
SEQ = 1024
TILES = SEQ // P
NB, NT = 8, 4
NS = NB * NT
NC = 1 + NB
H, DH, DV = 4, 64, 128
AW = H * DV
PAGES = 32
POOL = 320
PAST = PAGES * P
CONV = 3
BUCKETS, MAX_DIST = 32, 128
PH, PK, TOPK = 8, 128, 16
HP = 2 * PH
SEL = PH * TOPK
ALPHA = 2.0 ** 0.25
EPS = 1e-5
LAM_INIT = 0.8 - 0.6 * math.exp(-0.3 * 0)
MASKED = -1e30
BANK = 512
STRIP = SEQ + P
TOEP = STRIP + P - 1
TAIL = P + NT
SHIFT1, SCALE1, GATE1, SHIFT2, SCALE2, GATE2 = range(6)
GROUP = 4
RING = 8


def take(eng, sem, n=1):
    eng.wait_ge(sem, n)
    eng.sem_inc(sem, -n)


class Steps:

    def __init__(self, eng, sem):
        self.eng, self.sem, self.n = eng, sem, 0

    def __call__(self, ins):
        ins.then_inc(self.sem, 1)
        self.n += 1

    def done(self):
        self.eng.wait_ge(self.sem, self.n)

    def reset(self):
        if self.n:
            self.done()
            self.eng.sem_inc(self.sem, -self.n)
            self.n = 0

    def tell(self, *sems):
        self.done()
        for s in sems:
            self.eng.sem_inc(s, 1)


def flat(ap):
    return ap.rearrange("p a n -> p (a n)")


def over(ap, n):
    return ap.unsqueeze(2).to_broadcast([ap.shape[0], ap.shape[1], n])


def build(nc, A):
    with ExitStack() as top:
        used = []

        def sem(name):
            used.append(nc.alloc_semaphore(name=name))
            return used[-1]

        def end_stage():
            nc.clear_and_free_semaphores(used)
            nc.all_engine_barrier()
            used.clear()

        def sbuf(stack, name, shape, dt=F32):
            return stack.enter_context(nc.sbuf_tensor("sb_" + name, shape, dt))

        psum = top.enter_context(nc.psum_tensor("psum", [P, 8, BANK], F32))
        toep_dram = nc.dram_tensor("toep_scratch", (H, P, TOEP), F32, kind="Internal").ap()
        x1_dram = nc.dram_tensor("x1_scratch", (SEQ + P, D), F32, kind="Internal").ap()
        mod_dram = nc.dram_tensor("mod_scratch", (NC, 6 * D), F32, kind="Internal").ap()
        h2_dram = nc.dram_tensor("h2_scratch", (SEQ + P, D), F32, kind="Internal").ap()

        ident = sbuf(top, "ident", [P, P])
        ones = sbuf(top, "ones", [P, P])
        gate2 = sbuf(top, "gate2", [P, 2, D])
        lam = sbuf(top, "lam", [P, 2])
        eps = sbuf(top, "eps", [P, 1])
        tensors = dict(nc=nc, A=A, sem=sem, sbuf=sbuf, psum=psum, toep_dram=toep_dram, x1_dram=x1_dram,
                       h2_dram=h2_dram, mod_dram=mod_dram, ident=ident, ones=ones, lam=lam, eps=eps, gate2=gate2)
        with ExitStack() as mid:
            tensors["modT"] = sbuf(mid, "modT", [P, 2, KD, NC])
            condition(**tensors)
            end_stage()
            o_att = sbuf(mid, "o_att", [P, TILES + 1, AW])
            o_convT = sbuf(mid, "o_convT", [P, H, SEQ + NS])
            zlast, zslast = sbuf(mid, "z_last", [P, H, 2]), sbuf(mid, "z_sample_last", [P, H, NB, 2])
            tensors |= dict(o_att=o_att, o_convT=o_convT, zlast=zlast, zslast=zslast)
            with ExitStack() as att:
                tensors |= dict(qT=sbuf(att, "qT", [P, H, SEQ + NS]), kT=sbuf(att, "kT", [P, H, SEQ + NS]),
                                v=sbuf(att, "v", [P, TILES + 1, AW]))
                project(**tensors)
                end_stage()
                prompt_attention(**tensors)
                end_stage()
                sample_attention(**tensors)
                end_stage()
            mix(**tensors)
            end_stage()
        peer(**tensors)


def condition(nc, A, sem, sbuf, psum, mod_dram, toep_dram, ident, ones, modT, lam, eps, **_):
    NBLK, SL = 12, 3
    with ExitStack() as st:
        w = sbuf(st, "w_ada", [P, SL, KD, BANK])
        b = sbuf(st, "b_ada", [1, SL, BANK])
        mod = sbuf(st, "mod", [NC, 6 * D])
        c = sbuf(st, "c", [NC, D])
        cs = sbuf(st, "c_silu", [NC, D])
        cT = sbuf(st, "cT", [P, KD, NC])
        lq = sbuf(st, "lq", [1, 4, DH])
        lw = sbuf(st, "lw", [1, 8])
        rel = sbuf(st, "rel_bias", [BUCKETS + 1, H])
        relw = sbuf(st, "rel_wide", [BUCKETS + 1, H, P])
        hot = sbuf(st, "onehot", [BUCKETS + 1, TOEP])
        bias_rows = sbuf(st, "bias_rows", [P, H, TOEP])
        rel_land, rel_wide, bias_psum, bias_copied, bias_stored = (sem("tp_" + n) for n in
                                                                   "rel_land rel_wide psum copied stored".split())
        cuts = [(a, min(BANK, TOEP - a)) for a in range(0, TOEP, BANK)]
        BIAS = (5, 0)
        consts = sem("consts")
        w_land, w_free = ([sem(f"w_ada_{what}{u}") for u in range(SL)] for what in ("land", "free"))
        silu, cT_psum, cT_sbuf = sem("silu"), sem("cT_psum"), sem("cT_sbuf")
        m_psum, m_free = [sem(f"m_psum{u}") for u in range(2)], [sem(f"m_free{u}") for u in range(2)]
        mod_ready, modT_psum, lam_exp, lam_arg, lam_bc, lam_row = (sem("mod_ready"), sem("modT_psum"), sem("lam_exp"),
                                                                  sem("lam_arg"), sem("lam_bc"), sem("lam_row"))
        dve_c, act_c, ones_ready, mod_stored = sem("dve_c"), sem("act_c"), sem("ones_ready"), sem("mod_stored")
        w_v = A["w_ada"][0].rearrange("(k p) n -> p k n", p=P)
        with nc.Block() as block:
            @block.sync
            def _(sp):
                sp.dma_start(rel[0:BUCKETS, :], A["rel_bias"]).then_inc(rel_land, 16)
                sp.dma_start(hot[:], A["const_onehot"]).then_inc(rel_land, 16)
                sp.dma_start(c[0:1, :], A["c_prompt"]).then_inc(consts, 16)
                sp.dma_start(c[1:NC, :], A["c_sample"]).then_inc(consts, 16)
                sp.dma_start(ident[:], A["const_ident"]).then_inc(consts, 16)
                for n, name in enumerate(("lambda_q1", "lambda_k1", "lambda_q2", "lambda_k2")):
                    sp.dma_start(lq[:, n, :], A[name]).then_inc(consts, 16)
                with sp.Fori(0, NBLK // SL) as i:
                    for u in range(SL):
                        take(sp, w_free[u])
                        sp.dma_start(w[:, u], w_v[:, :, ds((i * SL + u) * BANK, BANK)]).then_inc(w_land[u], 16)
                        sp.dma_start(b[:, u, :], A["b_ada"][:, ds((i * SL + u) * BANK, BANK)]).then_inc(w_land[u], 16)
                sp.wait_ge(mod_ready, 1)
                sp.dma_start(mod_dram, mod[:]).then_inc(mod_stored, 16)
                sp.wait_ge(mod_stored, 16)

            @block.scalar
            def _(act):
                act.wait_ge(consts, 7 * 16)
                nc.scalar.activation(cs[:], c[:], ACT.Silu).then_inc(silu, 1)
                for h in range(H):
                    act.wait_ge(bias_copied, h + 1)
                    act.dma_start(toep_dram[h], bias_rows[:, h, :]).then_inc(bias_stored, 16)
                act.wait_ge(cT_psum, 1)
                nc.scalar.copy(cT[:], psum[:, 2, 0:KD * NC].rearrange("p (k c) -> p k c", k=KD)).then_inc(cT_sbuf, 1)
                with act.Fori(0, NBLK // 6) as i:
                    for n in range(6):
                        take(act, m_psum[n % 2])
                        act.sem_inc(w_free[n % SL], 1)
                        nc.scalar.copy(mod[:, ds((i * 6 + n) * BANK, BANK)], psum[0:NC, n % 2, :]).then_inc(m_free[n % 2], 1)
                act.wait_ge(lam_arg, 1)
                nc.scalar.activation(lw[:, 2:4], lw[:, 0:2], ACT.Exp).then_inc(lam_exp, 1)
                act.wait_ge(bias_stored, 16 * H)

            @block.tensor
            def _(pe):
                for u in range(SL):
                    pe.sem_inc(w_free[u], 1)
                pe.wait_ge(rel_wide, 1)
                pe.wait_ge(rel_land, 32)
                for h in range(H):
                    if h >= 2:
                        pe.wait_ge(bias_copied, h - 1)
                    for n, (a, width) in enumerate(cuts):
                        ins = nc.tensor.matmul(psum[:, BIAS[h % 2] + n, 0:width], relw[:, h, :], hot[:, a:a + width],
                                               start=True, stop=True)
                    ins.then_inc(bias_psum, 1)
                pe.wait_ge(consts, 7 * 16)
                pe.wait_ge(silu, 1)
                pe.wait_ge(bias_copied, H)
                for k in range(KD):
                    ins = nc.tensor.transpose(psum[:, 2, k * NC:(k + 1) * NC], cs[:, k * P:(k + 1) * P], ident[0:NC, 0:NC])
                ins.then_inc(cT_psum, 1)
                pe.wait_ge(cT_sbuf, 1)
                pe.wait_ge(ones_ready, 1)
                for u in range(2):
                    pe.sem_inc(m_free[u], 1)
                with pe.Fori(0, NBLK // 6) as i:
                    for n in range(6):
                        u, m = n % SL, n % 2
                        take(pe, w_land[u], 32)
                        take(pe, m_free[m])
                        for k in range(KD):
                            nc.tensor.matmul(psum[0:NC, m, :], cT[:, k, :], w[:, u, k, :], start=(k == 0), stop=False)
                        nc.tensor.matmul(psum[0:NC, m, :], ones[0:1, 0:NC], b[:, u, :],
                                         start=False, stop=True).then_inc(m_psum[m], 1)
                for m in range(2):
                    take(pe, m_free[m])
                pe.sem_inc(mod_ready, 1)
                for q, kind in enumerate((SHIFT1, SCALE1)):
                    for k in range(KD):
                        ins = nc.tensor.transpose(psum[:, 3, (q * KD + k) * NC:(q * KD + k + 1) * NC],
                                                  mod[:, kind * D + k * P:kind * D + (k + 1) * P], ident[0:NC, 0:NC])
                ins.then_inc(modT_psum, 1)
                pe.wait_ge(lam_row, 1)
                nc.tensor.matmul(psum[:, 4, 0:1], ones[0:1, :], lw[:, 4:5], start=True, stop=True).then_inc(lam_bc, 1)

            @block.vector
            def _(dve):
                step = Steps(dve, dve_c)
                step(nc.vector.memset(rel[BUCKETS:BUCKETS + 1, :], MASKED))
                dve.wait_ge(rel_land, 32)
                step.done()
                step(nc.vector.tensor_copy(relw[:], over(rel[:], P)))
                step.tell(rel_wide)
                for h in range(H):
                    dve.wait_ge(bias_psum, h + 1)
                    f = psum[:, BIAS[h % 2]:BIAS[h % 2] + 3, :].rearrange("p b n -> p (b n)")[:, 0:TOEP]
                    step(nc.vector.tensor_copy(bias_rows[:, h, :], f))
                    step.tell(bias_copied)
                step(nc.vector.memset(ones[:], 1.0))
                step(nc.vector.memset(eps[:], EPS))
                step.tell(ones_ready)
                dve.wait_ge(consts, 7 * 16)
                for n in range(2):
                    step(nc.vector.tensor_tensor_reduce(lq[:, 2 * n, :], lq[:, 2 * n, :], lq[:, 2 * n + 1, :], 1.0, 0.0,
                                                        ALU.mult, ALU.add, lw[:, n:n + 1]))
                step.tell(lam_arg)
                dve.wait_ge(lam_exp, 1)
                step(nc.vector.tensor_tensor(lw[:, 5:6], lw[:, 2:3], lw[:, 3:4], ALU.subtract))
                step.done()
                step(nc.vector.tensor_scalar(lw[:, 4:5], lw[:, 5:6], LAM_INIT, None, ALU.add))
                step.tell(lam_row)
                dve.wait_ge(modT_psum, 1)
                for q in range(2):
                    step(nc.vector.tensor_scalar(modT[:, q], psum[:, 3, q * KD * NC:(q + 1) * KD * NC].rearrange(
                        "p (k c) -> p k c", k=KD), float(q % 2), None, ALU.add))
                dve.wait_ge(lam_bc, 1)
                step(nc.vector.tensor_copy(lam[:, 0:1], psum[:, 4, 0:1]))
                step(nc.vector.tensor_scalar(lam[:, 1:2], psum[:, 4, 0:1], -1.0, None, ALU.mult))
                step.done()


def project(nc, A, sem, sbuf, psum, ident, modT, qT, kT, v, o_convT, zlast, zslast, **_):
    with ExitStack() as outer, ExitStack() as st:
        hT = sbuf(outer, "hT", [P, KD, SEQ + NS])
        w = sbuf(st, "w_qkv", [P, KD, 3 * AW])
        x = sbuf(st, "x_in", [P, 2, D])
        hTt = sbuf(st, "hT_tile", [P, 2, KD, P])
        qk = sbuf(st, "qk_tile", [P, 2, 2 * AW])
        vo = sbuf(st, "v_tile", [P, 2, AW])
        w_land = [sem(f"pj_w_land{j}") for j in range(3)]
        D2 = {n: [sem(f"pj_{n}{u}") for u in range(2)] for n in
              ("x_land", "x_free", "xT_ready", "hT_ready", "proj_ready", "qk_ready", "stored", "qkT_psum",
               "xT_free", "qkT_free", "proj_free")}
        act_c, dve_c = sem("pj_act_c"), sem("pj_dve_c")
        w_v = A["w_in"][0].rearrange("(k p) n -> p k n", p=P)
        x_t = A["x_prompt"][0].rearrange("(t p) d -> p t d", p=P)
        k_out = A["new_k_prompt"][0, 0].rearrange("(t p) h m d -> p t (h m d)", p=P)
        v_out = A["new_v_prompt"][0, 0].rearrange("(t p) h d -> p t (h d)", p=P)
        ks_out = A["new_k_sample"][0].rearrange("b t h m d -> (b t) (h m d)")
        vs_out = A["new_v_sample"][0].rearrange("b t h d -> (b t) (h d)")
        xs = A["x_sample"].rearrange("b t d -> (b t) d")

        def tiles(eng, body):
            with eng.Fori(0, TILES // 2) as i:
                for u in range(2):
                    body(u, i * 2 + u)
            body(0, None)

        with nc.Block() as block:
            @block.sync
            def _(sp):
                def body(u, t):
                    take(sp, D2["x_free"][u])
                    if t is None:
                        sp.dma_start(x[0:NS, u, :], xs).then_inc(D2["x_land"][u], 16)
                    else:
                        sp.dma_start(x[:, u, :], flat(x_t[:, ds(t, 1), :])).then_inc(D2["x_land"][u], 16)
                tiles(sp, body)

            @block.tensor
            def _(pe):
                for u in range(2):
                    pe.sem_inc(D2["x_free"][u], 1)

                def turn(u, t):
                    n = NS if t is None else P
                    take(pe, D2["x_land"][u], 16)
                    take(pe, D2["xT_free"][0])
                    for k in range(KD):
                        ins = nc.tensor.transpose(psum[:, k // 4, (k % 4) * P:(k % 4) * P + n],
                                                  x[0:n, u, k * P:(k + 1) * P], ident[0:n, 0:n])
                    ins.then_inc(D2["xT_ready"][0], 1)

                def products(u, t):
                    n = NS if t is None else P
                    take(pe, D2["hT_ready"][u])
                    for j in range(3):
                        pe.wait_ge(w_land[j], 16)
                        take(pe, D2["proj_free"][0])
                        for k in range(KD):
                            ins = nc.tensor.matmul(psum[0:n, 2 + j, :], hTt[:, u, k, 0:n], w[:, k, j * AW:(j + 1) * AW],
                                                   start=(k == 0), stop=(k == KD - 1))
                        ins.then_inc(D2["proj_ready"][0], 1)
                    take(pe, D2["qk_ready"][u])
                    take(pe, D2["qkT_free"][0])
                    for j in range(2 * H):
                        ins = nc.tensor.transpose(psum[:, 5 + j // 4, (j % 4) * P:(j % 4) * P + n],
                                                  qk[0:n, u, j * P:(j + 1) * P], ident[0:n, 0:n])
                    ins.then_inc(D2["qkT_psum"][0], 1)

                turn(0, 0)
                with pe.Fori(0, TILES // 2 - 1) as i:
                    for u in range(2):
                        turn(1 - u, i * 2 + (u + 1))
                        products(u, i * 2 + u)
                for t in (TILES - 2, TILES - 1):
                    turn(1 - t % 2, t + 1 if t + 1 < TILES else None)
                    products(t % 2, t)
                products(0, None)

            @block.scalar
            def _(act):
                step = Steps(act, act_c)
                for j in range(3):
                    cols = slice(j * AW, (j + 1) * AW)
                    act.dma_start(w[:, :, cols], w_v[:, :, cols]).then_inc(w_land[j], 16)
                act.sem_inc(D2["qkT_free"][0], 1)
                act.sem_inc(D2["proj_free"][0], 3)

                def body(u, t):
                    n = NS if t is None else P
                    at = SEQ if t is None else t * P
                    for j in range(3):
                        take(act, D2["proj_ready"][0])
                        if j == 0:
                            take(act, D2["stored"][u], 32)
                        if j < 2:
                            step(nc.scalar.copy(qk[0:n, u, j * AW:(j + 1) * AW], psum[0:n, 2 + j, :]))
                        else:
                            step(nc.scalar.copy(vo[0:n, u, :], psum[0:n, 2 + j, :]))
                        step.tell(D2["proj_free"][0])
                        if j == 1:
                            act.sem_inc(D2["qk_ready"][u], 1)
                    if t is None:
                        act.dma_start(ks_out, qk[0:NS, u, AW:2 * AW]).then_inc(D2["stored"][u], 16)
                        act.dma_start(vs_out, vo[0:NS, u, :]).then_inc(D2["stored"][u], 16)
                        step(nc.scalar.copy(v[0:NS, TILES, :], vo[0:NS, u, :]))
                    else:
                        act.dma_start(flat(k_out[:, ds(t, 1), :]), qk[:, u, AW:2 * AW]).then_inc(D2["stored"][u], 16)
                        act.dma_start(flat(v_out[:, ds(t, 1), :]), vo[:, u, :]).then_inc(D2["stored"][u], 16)
                        step(nc.scalar.copy(flat(v[:, ds(t, 1), :]), vo[:, u, :]))
                    take(act, D2["qkT_psum"][0])
                    src = psum[:, 5:7, :].rearrange("p b (h n) -> p b h n", h=H)
                    step(nc.scalar.mul(qT[:, :, ds(at, n)], src[:, 0, :, 0:n], DH ** -0.5))
                    step(nc.scalar.copy(kT[:, :, ds(at, n)], src[:, 1, :, 0:n]))
                    step.tell(D2["qkT_free"][0])
                    step.reset()

                for u in range(2):
                    act.sem_inc(D2["stored"][u], 32)
                tiles(act, body)
                for u in range(2):
                    act.wait_ge(D2["stored"][u], 32)

            @block.vector
            def _(dve):
                step = Steps(dve, dve_c)
                dve.sem_inc(D2["xT_free"][0], 1)

                def body(u, t):
                    take(dve, D2["xT_ready"][0])
                    if t is not None:
                        for k in range(KD):
                            src = psum[:, k // 4, (k % 4) * P:(k % 4 + 1) * P]
                            step(nc.vector.tensor_scalar(hTt[:, u, k, :], src, modT[:, 1, k, 0:1], modT[:, 0, k, 0:1],
                                                         ALU.mult, ALU.add))
                        step.tell(D2["hT_ready"][u], D2["xT_free"][0], D2["x_free"][u])
                        step(nc.vector.tensor_copy(hT[:, :, ds(t * P, P)], hTt[:, u]))
                    else:
                        for k in range(KD):
                            src = psum[:, k // 4, (k % 4) * P:(k % 4) * P + NS].rearrange("p (b t) -> p b t", t=NT)
                            dst = hTt[:, u, k, 0:NS].rearrange("p (b t) -> p b t", t=NT)
                            step(nc.vector.tensor_tensor(dst, src, over(modT[:, 1, k, 1:NC], NT), ALU.mult))
                        step.done()
                        for k in range(KD):
                            dst = hTt[:, u, k, 0:NS].rearrange("p (b t) -> p b t", t=NT)
                            step(nc.vector.tensor_tensor(dst, dst, over(modT[:, 0, k, 1:NC], NT), ALU.add))
                        step.tell(D2["hT_ready"][u], D2["xT_free"][0])
                        step(nc.vector.tensor_copy(hT[:, :, SEQ:SEQ + NS], hTt[:, u, :, 0:NS]))
                    step.reset()
                tiles(dve, body)

        st.close()
        conv(nc, A, sem, sbuf, psum, hT, o_convT, zlast, zslast)


def conv(nc, A, sem, sbuf, psum, hT, o_convT, zlast, zslast):
    with ExitStack() as st:
        w = sbuf(st, "w_bcu", [P, 2, 3, KD, P])
        cw = sbuf(st, "conv_w", [P, H, CONV])
        cwc = sbuf(st, "conv_w_now", [P, CONV])
        pre = sbuf(st, "conv_prefix", [P, H, NB, 2])
        gc = sbuf(st, "gate_c", [P, SEQ + NS])
        z = sbuf(st, "z", [P, 2 + SEQ])
        zs = sbuf(st, "z_sample", [P, NB, 2 + NT])
        y = sbuf(st, "conv_y", [P, SEQ + NS])
        land = [[sem(f"cv_w_land{u}{j}") for j in range(3)] for u in range(2)]
        free = [sem(f"cv_w_free{u}") for u in range(2)]
        small = sem("cv_small")
        psum_ready, psum_free, gc_ready, gc_free = sem("cv_psum_ready"), sem("cv_psum_free"), sem("cv_gc_ready"), sem("cv_gc_free")
        dve_c = sem("cv_dve")
        w_v = A["w_in"][0].rearrange("(k p) n -> p k n", p=P)
        N = (SEQ + NS) // 3
        PARTS = ((0, N), (N, N), (2 * N, N))
        COL = (4 * AW, 5 * AW, 3 * AW)

        def where(u, part, j):
            return psum[:, 3 * ((3 * u + part) % 2) + j, 0:N]

        def blocks(eng, body):
            with eng.Fori(0, H // 2) as i:
                for u in range(2):
                    body(u, i * 2 + u)

        with nc.Block() as block:
            @block.sync
            def _(sp):
                with sp.Fori(0, H // 2) as i:
                    for u in range(2):
                        take(sp, free[u])
                        for j in range(3):
                            sp.dma_start(w[:, u, j], w_v[:, :, ds((i * 2 + u) * P + COL[j], P)]).then_inc(land[u][j], 16)

            @block.tensor
            def _(pe):
                for u in range(2):
                    pe.sem_inc(free[u], 1)

                def body(u, c):
                    for part, (at, n) in enumerate(PARTS):
                        take(pe, psum_free)
                        for j in range(3):
                            if part == 0:
                                take(pe, land[u][j], 16)
                            for k in range(KD):
                                ins = nc.tensor.matmul(where(u, part, j), w[:, u, j, k, :], hT[:, k, at:at + n],
                                                       start=(k == 0), stop=(k == KD - 1))
                        ins.then_inc(psum_ready, 1)
                blocks(pe, body)

            @block.scalar
            def _(act):
                with nc.allow_non_contiguous_dma("small"):
                    for j in range(CONV):
                        act.dma_start(cw[:, :, j], A["conv_w"][0, j].rearrange("(c p) -> p c", p=P)).then_inc(small, 16)
                    for b in range(NB):
                        for r in range(2):
                            act.dma_start(pre[:, :, b, r], A["state_conv"][0, b, r].rearrange("(c p) -> p c", p=P)).then_inc(small, 16)

                def body(u, c):
                    for part, (at, n) in enumerate(PARTS):
                        take(act, psum_ready)
                        if part == 2:
                            act.sem_inc(free[u], 1)
                        take(act, gc_free)
                        nc.scalar.copy(gc[:, at:at + n], where(u, part, 0)).then_inc(gc_ready, 1)
                blocks(act, body)

            @block.vector
            def _(dve):
                step = Steps(dve, dve_c)
                dve.sem_inc(psum_free, 2)
                dve.sem_inc(gc_free, 3)
                dve.wait_ge(small, 16 * (CONV + 2 * NB))
                step(nc.vector.memset(z[:, 0:2], 0.0))
                step.reset()

                def gated(new, c_in, u_in, b_in, old, y_p, dst):
                    step(nc.vector.tensor_tensor(new, c_in, u_in, ALU.mult))
                    step.done()
                    step(nc.vector.tensor_scalar(y_p, old[0], cwc[:, 0:1], None, ALU.mult))
                    for j in (1, 2):
                        step.done()
                        step(nc.vector.scalar_tensor_tensor(out=y_p, in0=old[j], scalar=cwc[:, j:j + 1], in1=y_p,
                                                            op0=ALU.mult, op1=ALU.add))
                    step.done()
                    step(nc.vector.tensor_tensor(dst, y_p, b_in, ALU.mult))

                def body(u, c):
                    step(nc.vector.tensor_copy(cwc[:], flat(cw[:, ds(c, 1), :])))
                    step(nc.vector.tensor_copy(zs[:, :, 0:2], pre[:, ds(c, 1)].rearrange("p a b r -> p (a b) r")))
                    for part, (at, n) in enumerate(PARTS):
                        take(dve, gc_ready)
                        many = min(n, SEQ - at)
                        gc_p, u_p, b_p = gc[:, at:at + many], where(u, part, 1)[:, 0:many], where(u, part, 2)[:, 0:many]
                        gated(z[:, 2 + at:2 + at + many], gc_p, u_p, b_p, [z[:, at + j:at + j + many] for j in range(CONV)],
                              y[:, at:at + many], o_convT[:, ds(c, 1), at:at + many].rearrange("p a n -> p (a n)"))
                        if many < n:
                            split = lambda ap: ap.rearrange("p (b t) -> p b t", t=NT)
                            step.done()
                            gated(zs[:, :, 2:], split(gc[:, SEQ:]), split(where(u, part, 1)[:, many:n]),
                                  split(where(u, part, 2)[:, many:n]), [zs[:, :, j:j + NT] for j in range(CONV)],
                                  split(y[:, SEQ:]), split(o_convT[:, ds(c, 1), SEQ:].rearrange("p a n -> p (a n)")))
                        step.tell(psum_free, gc_free)
                    step(nc.vector.tensor_copy(flat(zlast[:, ds(c, 1), :]), z[:, SEQ:SEQ + 2]))
                    step(nc.vector.tensor_copy(zslast[:, ds(c, 1)].rearrange("p a b r -> p (a b) r"), zs[:, :, NT:NT + 2]))
                    step.reset()
                blocks(dve, body)


def prompt_attention(nc, A, sem, sbuf, psum, toep_dram, ident, ones, lam, qT, kT, v, o_att, zlast, zslast, **_):
    with ExitStack() as st:
        strip = sbuf(st, "bias_strip", [P, H, STRIP])
        e = sbuf(st, "scores", [P, 3, 2, SEQ])
        wgt = sbuf(st, "weights", [P, SEQ])
        wT = sbuf(st, "weightsT", [P, 2, TILES, P])
        mx, nmx, z = (sbuf(st, n, [P, 3, 2]) for n in ("row_max", "neg_max", "row_sum"))
        rz = sbuf(st, "row_scale", [P, 2])
        T = {n: sem("at_" + n) for n in
             "s_ready s_free e_ready p_ready w_ready w_free wT_psum wT_free wT_ready o_ready o_free".split()}
        dve_c, act_c, strip_land, state_stored = sem("at_dve"), sem("at_act"), sem("at_strip"), sem("at_state_stored")

        def heads(*parts):
            for k in range(-2, TILES * H):
                for ahead, part in parts:
                    if 0 <= k + ahead < TILES * H:
                        part(k + ahead, (k + ahead) // H, (k + ahead) % H)

        with nc.Block() as block:
            @block.sync
            def _(sp):
                for h in range(H):
                    f = toep_dram[h].rearrange("q m -> (q m)")[P - 1:P - 1 + P * (TOEP - 1)]
                    sp.dma_start(strip[:, h, :], f.rearrange("(q m) -> q m", q=P)[:, 0:STRIP]).then_inc(strip_land, 16)
                with nc.allow_non_contiguous_dma("small"):
                    for r in range(2):
                        sp.dma_start(A["new_conv_prompt"][0, 0, r].rearrange("(c p) -> p c", p=P), zlast[:, :, r]).then_inc(state_stored, 16)
                        for b in range(NB):
                            sp.dma_start(A["new_conv_sample"][0, b, r].rearrange("(c p) -> p c", p=P),
                                         zslast[:, :, b, r]).then_inc(state_stored, 16)
                sp.wait_ge(state_stored, 16 * 2 * (1 + NB))

            @block.tensor
            def _(pe):
                pe.sem_inc(T["s_free"], 1)
                pe.sem_inc(T["w_free"], 1)
                pe.sem_inc(T["wT_free"], 1)
                pe.sem_inc(T["o_free"], 2)

                def scores(k, t, h):
                    keys = (t + 1) * P
                    take(pe, T["s_free"])
                    for m in range(2):
                        rows = slice(m * DH, (m + 1) * DH)
                        for b, at in enumerate(range(0, keys, BANK)):
                            n = min(BANK, keys - at)
                            ins = nc.tensor.matmul(psum[:, 2 * m + b, 0:n], qT[rows, h, t * P:(t + 1) * P],
                                                   kT[rows, h, at:at + n], start=True, stop=True)
                    ins.then_inc(T["s_ready"], 1)

                def turn(k, t, h):
                    take(pe, T["w_ready"])
                    take(pe, T["wT_free"])
                    for j in range(t + 1):
                        ins = nc.tensor.transpose(psum[:, 4 + j // 4, (j % 4) * P:(j % 4 + 1) * P],
                                                  wgt[:, j * P:(j + 1) * P], ident[:])
                    ins.then_inc(T["wT_psum"], 1)

                def values(k, t, h):
                    take(pe, T["wT_ready"])
                    if h == 0:
                        take(pe, T["o_free"])
                    for j in range(t + 1):
                        ins = nc.tensor.matmul(psum[:, 6 + t % 2, h * DV:(h + 1) * DV], wT[:, k % 2, j, :],
                                               v[:, j, h * DV:(h + 1) * DV], start=(j == 0), stop=(j == t))
                    if h == H - 1:
                        ins.then_inc(T["o_ready"], 1)
                heads((2, scores), (1, turn), (0, values))

            @block.vector
            def _(dve):
                step = Steps(dve, dve_c)
                dve.wait_ge(strip_land, 16 * H)

                def biased(k, t, h):
                    keys, u = (t + 1) * P, k % 3
                    bias = strip[:, h, SEQ - t * P:SEQ - t * P + keys]
                    take(dve, T["s_ready"])
                    for m in range(2):
                        step(nc.vector.tensor_tensor_reduce(
                            e[:, u, m, 0:keys], flat(psum[:, 2 * m:2 * m + 2, :])[:, 0:keys], bias, 1.0, MASKED,
                            ALU.add, ALU.max, mx[:, u, m:m + 1]))
                    step.done()
                    step(nc.vector.tensor_scalar(nmx[:, u, :], mx[:, u, :], -1.0, None, ALU.mult))
                    step.tell(T["e_ready"], T["s_free"])

                def combined(k, t, h):
                    keys, u = (t + 1) * P, k % 3
                    take(dve, T["p_ready"])
                    step(nc.vector.reciprocal(rz[:], z[:, u, :]))
                    step.done()
                    step(nc.vector.tensor_tensor(rz[:, 1:2], rz[:, 1:2], lam[:, 1:2], ALU.mult))
                    step.done()
                    step(nc.vector.tensor_scalar(e[:, u, 1, 0:keys], e[:, u, 1, 0:keys], rz[:, 1:2], None, ALU.mult))
                    step.done()
                    take(dve, T["w_free"])
                    step(nc.vector.scalar_tensor_tensor(out=wgt[:, 0:keys], in0=e[:, u, 0, 0:keys], scalar=rz[:, 0:1],
                                                        in1=e[:, u, 1, 0:keys], op0=ALU.mult, op1=ALU.add))
                    step.tell(T["w_ready"])
                    step.reset()
                heads((1, combined), (2, biased))

            @block.scalar
            def _(act):
                step = Steps(act, act_c)

                def exps(k, t, h):
                    keys, u = (t + 1) * P, k % 3
                    take(act, T["e_ready"])
                    for m in range(2):
                        step(nc.scalar.activation(e[:, u, m, 0:keys], e[:, u, m, 0:keys], ACT.Exp,
                                                  bias=nmx[:, u, m:m + 1], accum_out=z[:, u, m:m + 1]))
                    step.tell(T["p_ready"])

                def turned(k, t, h):
                    take(act, T["wT_psum"])
                    act.sem_inc(T["w_free"], 1)
                    step(nc.scalar.copy(wT[:, k % 2, 0:t + 1, :].rearrange("p j n -> p (j n)"),
                                        flat(psum[:, 4:6, :])[:, 0:(t + 1) * P]))
                    step.tell(T["wT_ready"], T["wT_free"])

                def output(k, t, h):
                    if h == H - 1:
                        take(act, T["o_ready"])
                        step(nc.scalar.copy(o_att[:, t, :], psum[:, 6 + t % 2, :]))
                        step.tell(T["o_free"])
                        step.reset()
                heads((1, turned), (2, exps), (0, output))


def sample_attention(nc, A, sem, sbuf, psum, ident, lam, qT, kT, v, o_att, **_):
    R = H * 2 * NT
    CH = 4
    NCH = PAGES // CH
    WROW = 2 + AW + NB * R
    with ExitStack() as st:
        pt = sbuf(st, "page_table", [1, NB * PAGES], I32)
        kp = sbuf(st, "k_pages", [P, 2, CH, AW])
        vp = sbuf(st, "v_pages", [P, 2, CH, AW])
        kpT = sbuf(st, "k_pagesT", [P, 2, H, CH * P])
        q_all = sbuf(st, "q_rows", [P, NB, H, R])
        q_now = sbuf(st, "q_rows_now", [P, H, R])
        rel = sbuf(st, "rel_bias_s", [BUCKETS + 1, H])
        relr = sbuf(st, "rel_rows", [BUCKETS + 1, NT, H, 2, NT])
        hot = sbuf(st, "onehot_tail", [BUCKETS + 1, NT, TAIL + 1])
        rows = sbuf(st, "row_consts", [R, WROW])
        tail = sbuf(st, "tail_bias", [R, TAIL])
        far = sbuf(st, "far_bias", [R, 1])
        coef = sbuf(st, "map_coef", [R, 1])
        vb = sbuf(st, "v_new", [NT, NB, AW])
        vb_now = sbuf(st, "v_new_now", [NT, AW])
        sc = sbuf(st, "scores_s", [R, PAST + NT])
        pT = sbuf(st, "probsT", [P, PAGES + 1, R])
        mx, nmx, rz = (sbuf(st, n, [R, 1]) for n in ("mx_s", "nmx_s", "rz_s"))
        mxs, z = sbuf(st, "mx_chunks", [R, NCH]), sbuf(st, "z_parts", [R, NCH // 2])
        ex = qT[0:R].rearrange("r h n -> r (h n)")
        comb = sbuf(st, "comb_now", [R, NS])
        om = sbuf(st, "o_masked", [R, AW])
        zero = sbuf(st, "zeros_s", [R, NS + AW])
        T = {n: sem("sa_" + n) for n in
             ("tab small q_ready bias_psum setup k_free0 k_free1 k_land0 k_land1 v_free0 v_free1 v_land0 v_land1 "
              "kT_act kT_dve kT_done_act kT_done_dve kT_free_act kT_free_dve s_ready s_free s_copied q_now max_ready "
              "exp_ready z_ready pT_psum pT_ready pT_free o_psum om_ready om_free sum_ready").split()}
        dve_c, act_c = sem("sa_dve"), sem("sa_act")

        EXPS, VSLOT = NCH // 2, 3

        def exp_cols(p):
            return slice(p * 2 * BANK, (p + 1) * 2 * BANK + (NT if p == EXPS - 1 else 0))

        def samples(eng, body):
            body(0, None)
            with eng.Fori(0, NB - 1) as i:
                body(i + 1, i)
            body(None, NB - 1)

        with nc.Block() as block:
            @block.sync
            def _(sp):
                sp.dma_start(pt[:], A["page_table"].rearrange("(a b) n -> a (b n)", a=1)).then_inc(T["tab"], 16)
                sp.dma_start(rel[0:BUCKETS, :], A["rel_bias"]).then_inc(T["small"], 16)
                sp.dma_start(hot[:], A["const_tail"]).then_inc(T["small"], 16)
                sp.dma_start(rows[:], A["const_rows"]).then_inc(T["small"], 16)
                for b in range(NB):
                    sp.dma_start(vb[:, b, :], v[b * NT:(b + 1) * NT, TILES, :]).then_inc(T["small"], 16)
                sp.wait_ge(T["tab"], 16)
                cache_k = A["cache_k"][0].rearrange("g p h m d -> g p (h m d)")
                cache_v = A["cache_v"][0].rearrange("g p h d -> g p (h d)")

                def load(cache, slots, x, b, c):
                    u = c % 2
                    pages = [sp.value_load(pt[0:1, ds(b * PAGES + (c * CH + g), 1)], min_val=0, max_val=POOL - 1)
                             for g in range(CH)]
                    take(sp, T[f"{x}_free{u}"])
                    for g, page in enumerate(pages):
                        sp.dma_start(slots[:, u, g, :], cache[ds(page, 1)].rearrange("a p n -> (a p) n"))\
                            .then_inc(T[f"{x}_land{u}"], 16)

                def body(b, prev):
                    for c in range(NCH):
                        if b is not None:
                            load(cache_k, kp, "k", b, c)
                        if prev is not None and c >= NCH // 2:
                            for j in range(2):
                                load(cache_v, vp, "v", prev, 2 * (c - NCH // 2) + j)
                samples(sp, body)

            @block.tensor
            def _(pe):
                for x in "kv":
                    for u in range(2):
                        pe.sem_inc(T[f"{x}_free{u}"], 1)
                pe.sem_inc(T["kT_free_act"], 2)
                pe.sem_inc(T["kT_free_dve"], 2)
                pe.sem_inc(T["s_free"], 1)
                pe.sem_inc(T["pT_free"], 1)
                pe.sem_inc(T["om_free"], 1)
                pe.wait_ge(T["q_ready"], 1)
                for t in range(NT):
                    ins = nc.tensor.matmul(psum[0:R, 0, 0:TAIL + 1], relr[:, t].rearrange("p h m t -> p (h m t)"), hot[:, t, :],
                                           start=(t == 0), stop=(t == NT - 1))
                ins.then_inc(T["bias_psum"], 1)
                pe.wait_ge(T["setup"], 1)
                nc.tensor.matmul(psum[0:NS, 6, :], zero[:, 0:NS], zero[:, NS:], start=True, stop=False, skip_group_check=True)

                def turn_keys(c):
                    u = c % 2
                    take(pe, T[f"k_land{u}"], 16 * CH)
                    for h in range(H):
                        who = "act" if h % 2 else "dve"
                        take(pe, T[f"kT_free_{who}"])
                        for g in range(CH):
                            ins = nc.tensor.transpose(psum[:, h, g * P:(g + 1) * P], kp[:, u, g, h * P:(h + 1) * P], ident[:])
                        ins.then_inc(T[f"kT_{who}"], 1)

                def score(c):
                    for h in range(H):
                        take(pe, T["kT_done_act" if h % 2 else "kT_done_dve"])
                        if h == 0:
                            take(pe, T["s_free"])
                        ins = nc.tensor.matmul(psum[0:R, 4, :], q_now[:, h, :], kpT[:, c % 2, h, :],
                                               start=(h == 0), stop=(h == H - 1))
                    ins.then_inc(T["s_ready"], 1)

                def score_new(b):
                    take(pe, T["s_free"])
                    for h in range(H):
                        ins = nc.tensor.matmul(psum[0:R, 4, 0:NT], q_now[:, h, :], kT[:, h, ds(b * NT + SEQ, NT)],
                                               start=(h == 0), stop=(h == H - 1))
                    ins.then_inc(T["s_ready"], 1)

                def turn_probs(g):
                    if g < EXPS:
                        take(pe, T["exp_ready"])
                    take(pe, T["pT_free"])
                    for j in range(8 if g < EXPS else 1):
                        at = (g * 8 + j) * P
                        n = P if g < EXPS else NT
                        col = j * R
                        ins = nc.tensor.transpose(psum[0:n, 5, col:col + R], ex[:, at:at + n], ident[0:R, 0:R])
                    ins.then_inc(T["pT_psum"], 1)

                def values(c):
                    take(pe, T[f"v_land{c % 2}"], 16 * CH)
                    if c % 2 == 0:
                        take(pe, T["pT_ready"])
                    for g in range(CH):
                        ins = nc.tensor.matmul(psum[0:R, 7, :], pT[:, c * CH + g, :], vp[:, c % 2, g, :],
                                               start=(c == 0 and g == 0), stop=False)
                    ins.then_inc(T[f"v_free{c % 2}"], 1)

                def body(b, prev):
                    if b is not None:
                        take(pe, T["q_now"])
                        turn_keys(0)
                    for c in range(NCH):
                        if b is not None:
                            if c + 1 < NCH:
                                turn_keys(c + 1)
                            score(c)
                        if prev is not None:
                            if 1 <= c <= EXPS + 1:
                                turn_probs(c - 1)
                            if VSLOT <= c < VSLOT + NCH // 2:
                                values(2 * (c - VSLOT))
                                values(2 * (c - VSLOT) + 1)
                            if c == VSLOT + NCH // 2 - 1:
                                take(pe, T["pT_ready"])
                                nc.tensor.matmul(psum[0:R, 7, :], pT[0:NT, PAGES, :], vb_now[:],
                                                 start=False, stop=True).then_inc(T["o_psum"], 1)
                    if b is not None:
                        score_new(b)
                    if prev is not None:
                        take(pe, T["om_ready"])
                        nc.tensor.matmul(psum[0:NS, 6, :], comb[:], om[:], start=False, stop=False,
                                         skip_group_check=True).then_inc(T["om_free"], 1)
                samples(pe, body)
                for u in range(2):
                    take(pe, T[f"v_free{u}"])
                    take(pe, T[f"k_free{u}"])

            @block.scalar
            def _(act):
                step = Steps(act, act_c)
                act.wait_ge(T["setup"], 1)

                def copy_keys(c):
                    for h in (1, 3):
                        take(act, T["kT_act"])
                        if h == 3:
                            act.sem_inc(T[f"k_free{c % 2}"], 1)
                        step(nc.scalar.copy(kpT[:, c % 2, h, :], psum[:, h, :]))
                        step.tell(T["kT_done_act"], T["kT_free_act"])

                def body(b, prev):
                    if b is not None:
                        copy_keys(0)
                    for c in range(NCH):
                        if b is not None and c + 1 < NCH:
                            copy_keys(c + 1)
                        if prev is not None and c < EXPS:
                            if c == 0:
                                take(act, T["max_ready"])
                            s = exp_cols(c)
                            step(nc.scalar.activation(ex[:, s], sc[:, s], ACT.Exp, bias=nmx[:], accum_out=z[:, c:c + 1]))
                            step.tell(*([T["exp_ready"]] + ([T["z_ready"]] if c == EXPS - 1 else [])))
                        if b is not None:
                            take(act, T["s_ready"])
                            step(nc.scalar.activation(sc[:, c * BANK:(c + 1) * BANK], psum[0:R, 4, :], ACT.Identity, bias=far[:]))
                            step.tell(T["s_free"], T["s_copied"])
                    if b is not None:
                        take(act, T["s_ready"])
                        step(nc.scalar.activation(sc[:, PAST:PAST + NT], psum[0:R, 4, 0:NT], ACT.Identity, bias=far[:]))
                        step.tell(T["s_free"], T["s_copied"])
                    step.reset()
                samples(act, body)
                act.wait_ge(T["sum_ready"], 1)
                nc.scalar.copy(o_att[0:NS, TILES, :], psum[0:NS, 6, :]).then_inc(act_c, 1)
                act.wait_ge(act_c, 1)

            @block.vector
            def _(dve):
                step = Steps(dve, dve_c)
                step(nc.vector.memset(rel[BUCKETS:BUCKETS + 1, :], MASKED))
                step(nc.vector.memset(relr[:], 0.0))
                step(nc.vector.memset(q_all[:], 0.0))
                step(nc.vector.memset(zero[:], 0.0))
                dve.wait_ge(T["small"], 16 * (3 + NB))
                step.done()
                for t in range(NT):
                    for m in range(2):
                        step(nc.vector.tensor_copy(relr[:, t, :, m, t], rel[:]))
                for h in range(H):
                    for m in range(2):
                        part = slice(m * DH, (m + 1) * DH)
                        r = h * 2 * NT + m * NT
                        step(nc.vector.tensor_copy(q_all[part, :, h, r:r + NT],
                                                   qT[part, h, SEQ:SEQ + NS].rearrange("p (b t) -> p b t", t=NT)))
                step.tell(T["q_ready"])
                dve.wait_ge(T["bias_psum"], 1)
                step(nc.vector.tensor_copy(far[:], psum[0:R, 0, TAIL:TAIL + 1]))
                step.done()
                step(nc.vector.tensor_scalar(tail[:], psum[0:R, 0, 0:TAIL], far[:], None, ALU.subtract))
                step(nc.vector.tensor_scalar(coef[:], rows[:, 1:2], lam[0:R, 1:2], rows[:, 0:1], ALU.mult, ALU.add))
                step.tell(T["setup"], T["setup"])
                step.reset()
                mask, combs = rows[:, 2:2 + AW], rows[:, 2 + AW:].rearrange("p (b n) -> p b n", b=NB)

                def copy_keys(c):
                    for h in (0, 2):
                        take(dve, T["kT_dve"])
                        step(nc.vector.tensor_copy(kpT[:, c % 2, h, :], psum[:, h, :]))
                        step.tell(T["kT_done_dve"], T["kT_free_dve"])

                def body(b, prev):
                    if b is not None:
                        step(nc.vector.tensor_copy(q_now[:], q_all[:, ds(b, 1)].rearrange("p a h r -> p (a h) r")))
                        step.tell(T["q_now"])
                        copy_keys(0)
                    if prev is not None:
                        step(nc.vector.tensor_copy(vb_now[:], vb[:, ds(prev, 1), :].rearrange("p a n -> p (a n)")))
                    for c in range(NCH):
                        if b is not None and c + 1 < NCH:
                            copy_keys(c + 1)
                        if b is not None:
                            take(dve, T["s_copied"])
                            if c < NCH - 1:
                                step(nc.vector.tensor_reduce(mxs[:, c:c + 1], sc[:, c * BANK:(c + 1) * BANK], AX, ALU.max))
                        if prev is not None and 1 <= c <= EXPS + 1:
                            take(dve, T["pT_psum"])
                            g = c - 1
                            if g < EXPS:
                                step(nc.vector.tensor_copy(pT[:, g * 8:(g + 1) * 8, :].rearrange("p g r -> p (g r)"),
                                                           psum[:, 5, 0:8 * R]))
                            else:
                                step(nc.vector.tensor_copy(pT[0:NT, PAGES, :], psum[0:NT, 5, 0:R]))
                            step.tell(T["pT_ready"], T["pT_free"])
                        if prev is not None and c == EXPS + 1:
                            take(dve, T["z_ready"])
                            step(nc.vector.tensor_reduce(rz[:], z[:], AX, ALU.add))
                            step.done()
                            step(nc.vector.reciprocal(rz[:], rz[:]))
                            step.done()
                            step(nc.vector.tensor_tensor(rz[:], rz[:], coef[:], ALU.mult))
                            step.done()
                            take(dve, T["om_free"])
                            step(nc.vector.tensor_scalar(comb[:], combs[:, ds(prev, 1), :].rearrange("p a n -> p (a n)"),
                                                         rz[:], None, ALU.mult))
                    if prev is not None:
                        take(dve, T["o_psum"])
                        step(nc.vector.tensor_tensor(om[:], psum[0:R, 7, :], mask, ALU.mult))
                        step.tell(T["om_ready"])
                    if b is not None:
                        take(dve, T["s_copied"])
                        step(nc.vector.tensor_tensor(sc[:, PAST - P:], sc[:, PAST - P:], tail[:], ALU.add))
                        step.done()
                        step(nc.vector.tensor_reduce(mxs[:, NCH - 1:NCH], sc[:, (NCH - 1) * BANK:], AX, ALU.max))
                        step.done()
                        step(nc.vector.tensor_reduce(mx[:], mxs[:], AX, ALU.max))
                        step.done()
                        step(nc.vector.tensor_scalar(nmx[:], mx[:], -1.0, None, ALU.mult))
                        step.tell(T["max_ready"])
                    step.reset()
                samples(dve, body)
                take(dve, T["om_free"])
                dve.sem_inc(T["sum_ready"], 1)


def mix(nc, A, sem, sbuf, psum, x1_dram, h2_dram, mod_dram, gate2, ident, eps, o_att, o_convT, **_):
    with ExitStack() as st:
        w = sbuf(st, "w_out", [P, KD, D])
        gate = sbuf(st, "gate1", [P, 2, D])
        sc2, sh2 = sbuf(st, "scale2", [P, 2, D]), sbuf(st, "shift2", [P, 2, D])
        lng = sbuf(st, "ln1", [P, 2, D])
        sub = sbuf(st, "subln", [P, DV])
        x = sbuf(st, "x_res", [P, 2, D])
        o_now = sbuf(st, "o_now", [P, 2, AW])
        c_now = sbuf(st, "oc_now", [P, 2, H, P])
        sq = sbuf(st, "o_sq", [P, 2, AW])
        oT = sbuf(st, "oT", [P, 2, H, P])
        ss, rt = sbuf(st, "ss", [P, H]), sbuf(st, "rt", [P, H])
        t1 = sbuf(st, "t1", [P, D])
        x1 = sbuf(st, "x1_out", [P, 2, D])
        h2 = sbuf(st, "h2_out", [P, 2, D])
        bn, ag, sd = sbuf(st, "bn1", [P, 2, 6]), sbuf(st, "ag1", [P, 2]), sbuf(st, "sd1", [P, 1])
        T = {n: sem("mx_" + n) for n in
             ("w_land small rows_land sub_ready staged o_free x_land0 x_land1 x_free0 x_free1 ss_ready rt_ready on_ready "
              "oT_psum oT_ready mix_psum mix_free var_ready sd_ready x1_ready0 x1_ready1 stored0 stored1").split()}
        TURN = (0, 5)
        dve_c, act_c, pool_c = sem("mx_dve"), sem("mx_act"), sem("mx_pool")
        x_t = A["x_prompt"][0].rearrange("(t p) d -> p t d", p=P)
        x1_t = x1_dram[0:SEQ, :].rearrange("(t p) d -> p t d", p=P)
        h2_t = h2_dram[0:SEQ, :].rearrange("(t p) d -> p t d", p=P)
        ROWS = []
        for kind, dst, copies in ((GATE1, gate, 1), (SCALE2, sc2, 1), (SHIFT2, sh2, 1), (GATE2, gate2, P // NS)):
            row = mod_dram[:, kind * D:(kind + 1) * D]
            ROWS.append((row[0:1, :].to_broadcast([P, D]), dst[:, 0]))
            for g in range(copies):
                ROWS.append((row[1:NC, :].unsqueeze(1).to_broadcast([NB, NT, D]), dst[g * NS:(g + 1) * NS, 1]))
        ROWS += [(A[name].to_broadcast([P, D]), lng[:, j]) for j, name in enumerate(("ln1_g", "ln1_b"))]

        def tiles(eng, ahead, rest, rest_first=False, between=lambda: None):
            def both(u, t, after):
                if rest_first:
                    rest(u, t)
                ahead(1 - u, after)
                if not rest_first:
                    rest(u, t)

            ahead(0, 0)
            between()
            with eng.Fori(0, TILES // 2 - 1) as i:
                for u in range(2):
                    both(u, i * 2 + u, i * 2 + (u + 1))
            for t in (TILES - 2, TILES - 1):
                both(t % 2, t, t + 1 if t + 1 < TILES else None)
            rest(0, None)

        def nothing(u, t):
            pass

        with nc.Block() as block:
            @block.sync
            def _(sp):
                sp.dma_start(sub[:], A["subln_w"].to_broadcast([P, DV])).then_inc(T["small"], 16)
                sp.dma_start(w[:], A["w_out"][0].rearrange("(k p) n -> p k n", p=P)).then_inc(T["w_land"], 16)

                def body(u, t):
                    take(sp, T[f"x_free{u}"])
                    if t is None:
                        sp.dma_start(x[0:NS, u, :], A["x_sample"].rearrange("b t d -> (b t) d")).then_inc(T[f"x_land{u}"], 16)
                    else:
                        sp.dma_start(x[:, u, :], flat(x_t[:, ds(t, 1), :])).then_inc(T[f"x_land{u}"], 16)
                tiles(sp, nothing, body)

            @block.gpsimd
            def _(pool):
                step = Steps(pool, pool_c)

                def body(u, t):
                    take(pool, T["o_free"])
                    if t is None:
                        step(nc.gpsimd.tensor_copy(o_now[0:NS, u, :], o_att[0:NS, TILES, :]))
                        step(nc.gpsimd.tensor_copy(c_now[:, u, :, 0:NS], o_convT[:, :, SEQ:SEQ + NS]))
                    else:
                        step(nc.gpsimd.tensor_copy(o_now[:, u, :], flat(o_att[:, ds(t, 1), :])))
                        step(nc.gpsimd.tensor_copy(c_now[:, u], o_convT[:, :, ds(t * P, P)]))
                    step.tell(T["staged"])
                    step.reset()
                tiles(pool, body, nothing)

            @block.tensor
            def _(pe):
                pe.sem_inc(T["o_free"], 2)
                pe.sem_inc(T["x_free0"], 1)
                pe.sem_inc(T["x_free1"], 1)
                pe.wait_ge(T["w_land"], 16)

                def turn(u, t):
                    n = NS if t is None else P
                    take(pe, T["on_ready"])
                    for h in range(H):
                        ins = nc.tensor.transpose(psum[:, TURN[u], h * P:h * P + n], sq[0:n, u, h * P:(h + 1) * P], ident[0:n, 0:n])
                    ins.then_inc(T["oT_psum"], 1)

                def product(u, t):
                    n = NS if t is None else P
                    take(pe, T["mix_free"])
                    take(pe, T["oT_ready"])
                    for k in range(KD):
                        lhsT = oT[:, u, k, 0:n] if k < H else c_now[:, u, k - H, 0:n]
                        for c in range(2):
                            ins = nc.tensor.matmul(psum[0:n, 1 + 2 * u + c, :], lhsT, w[:, k, c * BANK:(c + 1) * BANK],
                                                   start=(k == 0), stop=(k == KD - 1))
                    ins.then_inc(T["mix_psum"], 1)
                tiles(pe, turn, product, rest_first=True)

            @block.scalar
            def _(act):
                step = Steps(act, act_c)
                for src, dst in ROWS:
                    act.dma_start(dst, src).then_inc(T["rows_land"], 16)
                act.wait_ge(T["small"], 16)
                step(nc.scalar.mul(sub[:], sub[:], 1.0 - LAM_INIT))
                step.tell(T["sub_ready"])
                act.sem_inc(T["stored0"], 32)
                act.sem_inc(T["stored1"], 32)
                step.reset()

                def ahead(u, t):
                    n = NS if t is None else P
                    take(act, T["ss_ready"])
                    step(nc.scalar.activation(rt[0:n, :], ss[0:n, :], ACT.Sqrt, bias=eps[0:n, :], scale=1.0 / DV))
                    step.tell(T["rt_ready"])
                    take(act, T["oT_psum"])
                    step(nc.scalar.copy(oT[:, u, :, 0:n], psum[:, TURN[u], :].rearrange("p (h n) -> p h n", h=H)[:, :, 0:n]))
                    step.tell(T["oT_ready"])
                    step.reset()

                def rest(u, t):
                    n = NS if t is None else P
                    take(act, T["var_ready"])
                    step(nc.scalar.activation(sd[0:n, :], ag[0:n, 1:2], ACT.Sqrt, bias=eps[0:n, :]))
                    step.tell(T["sd_ready"])
                    take(act, T[f"x1_ready{u}"])
                    if t is None:
                        for g in range(P // NS):
                            rows = slice(SEQ + g * NS, SEQ + (g + 1) * NS)
                            act.dma_start(x1_dram[rows, :], x1[0:NS, u, :]).then_inc(T[f"stored{u}"], 16)
                            act.dma_start(h2_dram[rows, :], h2[0:NS, u, :]).then_inc(T[f"stored{u}"], 16)
                    else:
                        act.dma_start(flat(x1_t[:, ds(t, 1), :]), x1[:, u, :]).then_inc(T[f"stored{u}"], 16)
                        act.dma_start(flat(h2_t[:, ds(t, 1), :]), h2[:, u, :]).then_inc(T[f"stored{u}"], 16)
                    step.reset()
                tiles(act, ahead, rest)
                act.wait_ge(T["stored0"], 32 * (P // NS))
                act.wait_ge(T["stored1"], 32)

            @block.vector
            def _(dve):
                step = Steps(dve, dve_c)
                dve.sem_inc(T["mix_free"], 2)
                dve.wait_ge(T["sub_ready"], 1)

                def rows_landed():
                    dve.wait_ge(T["rows_land"], 16 * len(ROWS))
                    step(nc.vector.tensor_scalar(sc2[:, 0], sc2[:, 0], 1.0, None, ALU.add))
                    step(nc.vector.tensor_scalar(sc2[0:NS, 1], sc2[0:NS, 1], 1.0, None, ALU.add))
                    step.reset()

                def ahead(u, t):
                    n = NS if t is None else P
                    take(dve, T["staged"])
                    for h in range(H):
                        o = o_now[0:n, u, h * DV:(h + 1) * DV]
                        step(nc.vector.tensor_tensor_reduce(sq[0:n, u, h * DV:(h + 1) * DV], o, o, 1.0, 0.0, ALU.mult, ALU.add,
                                                            ss[0:n, h:h + 1]))
                    step.tell(T["ss_ready"])
                    take(dve, T["rt_ready"])
                    step(nc.vector.reciprocal(rt[0:n, :], rt[0:n, :]))
                    step.done()
                    for h in range(H):
                        s = slice(h * DV, (h + 1) * DV)
                        step(nc.vector.scalar_tensor_tensor(out=sq[0:n, u, s], in0=o_now[0:n, u, s], scalar=rt[0:n, h:h + 1],
                                                            in1=sub[0:n, :], op0=ALU.mult, op1=ALU.mult))
                    step.tell(T["on_ready"])
                    step.reset()

                def rest(u, t):
                    n = NS if t is None else P
                    take(dve, T["mix_psum"])
                    dve.sem_inc(T["o_free"], 1)
                    step(nc.vector.tensor_tensor(t1[0:n, :], flat(psum[0:n, 1 + 2 * u:3 + 2 * u, :]), gate[0:n, int(t is None), :], ALU.mult))
                    step.tell(T["mix_free"])
                    take(dve, T[f"x_land{u}"], 16)
                    step(nc.vector.scalar_tensor_tensor(out=t1[0:n, :], in0=x[0:n, u, :], scalar=ALPHA, in1=t1[0:n, :],
                                                        op0=ALU.mult, op1=ALU.add))
                    step.tell(T[f"x_free{u}"])
                    for c in range(2):
                        step(nc.vector.bn_stats(bn[0:n, c, :], t1[0:n, c * BANK:(c + 1) * BANK]))
                    step.done()
                    step(nc.vector.bn_aggr(ag[0:n, :], bn[0:n].rearrange("p a b -> p (a b)")))
                    step.tell(T["var_ready"])
                    take(dve, T["sd_ready"])
                    step(nc.vector.reciprocal(sd[0:n, :], sd[0:n, :]))
                    step.done()
                    step(nc.vector.tensor_scalar(t1[0:n, :], t1[0:n, :], ag[0:n, 0:1], sd[0:n, :], ALU.subtract, ALU.mult))
                    step.done()
                    step(nc.vector.tensor_tensor(t1[0:n, :], t1[0:n, :], lng[0:n, 0, :], ALU.mult))
                    step.done()
                    take(dve, T[f"stored{u}"], 32)
                    step(nc.vector.tensor_tensor(x1[0:n, u, :], t1[0:n, :], lng[0:n, 1, :], ALU.add))
                    step.done()
                    s = int(t is None)
                    step(nc.vector.tensor_tensor(h2[0:n, u, :], x1[0:n, u, :], sc2[0:n, s, :], ALU.mult))
                    step.done()
                    step(nc.vector.tensor_tensor(h2[0:n, u, :], h2[0:n, u, :], sh2[0:n, s, :], ALU.add))
                    step.tell(T[f"x1_ready{u}"])
                    step.reset()
                tiles(dve, ahead, rest, between=rows_landed)


def peer(nc, A, sem, sbuf, psum, x1_dram, h2_dram, ident, ones, eps, gate2, **_):
    GROUPS = SEL // GROUP
    PARTS = 4
    ALL = slice(0, PH)
    BESIDE_FIRST = {10: (0,), 11: (1,), 12: (2, 3), 13: (4, 5), 14: (6, 7), 15: (8, 9), 16: (10, 11), 17: (12,), 18: (13,),
                    19: (14, 15), 20: (16,), 21: (17,), 22: (18, 19), 23: (20,), 24: (21,), 25: (22, 23), 26: (24,),
                    27: (25,), 28: (26,), 29: (27, 28, 29)}
    COPIES = P // NS
    USES = SEL // RING
    with ExitStack() as st:
        w = sbuf(st, "w_pq", [P, KD, HP * P])
        subT = sbuf(st, "sub_keysT", [P, HP, PK])
        ring = sbuf(st, "ring", [P, RING, 2 * D])
        stage = sbuf(st, "index_stage", [P, 4, GROUP], U32)
        e_all = sbuf(st, "experts", [P, TILES + 1, SEL], U32)
        g_all = sbuf(st, "gates", [P, TILES + 1, SEL])
        h_sel = sbuf(st, "h2_next", [P, D])
        h_cur = sbuf(st, "h2_now", [P, D])
        hT = sbuf(st, "h2T", [P, KD, P])
        sc = sbuf(st, "scores_pk", [P, HP, PK])
        qT = sbuf(st, "queriesT", [P, HP, P])
        x_res = sbuf(st, "x1_res", [P, D])
        f = sbuf(st, "f", [P, D])
        lng = sbuf(st, "ln2", [P, 2, D])
        fold = sbuf(st, "fold", [P, P])
        diag = sbuf(st, "diag", [P, 2, GROUP, P])
        dots, act_g, wgt = (sbuf(st, n, [P, 2, GROUP]) for n in ("dots", "gelu", "expert_w"))
        sv, si, sif = sbuf(st, "sv", [P, 2, TOPK]), sbuf(st, "si", [P, 2, TOPK], U32), sbuf(st, "sif", [P, 2, TOPK])
        cand, iota, hot = sbuf(st, "cand", [P, TOPK, TOPK]), sbuf(st, "iota16", [P, TOPK]), sbuf(st, "hot", [P, TOPK, TOPK])
        cv = sbuf(st, "cv", [P, PH, TOPK])
        ci, cab, cabf = sbuf(st, "ci", [P, TOPK], U32), sbuf(st, "cab", [P, 2, TOPK], U32), sbuf(st, "cabf", [P, 2, TOPK])
        eab = sbuf(st, "eab", [P, 2, PH, TOPK])
        gsum = sbuf(st, "gsum", [P, PH])
        bn, ag, sd = sbuf(st, "bn2", [P, 2, 6]), sbuf(st, "ag2", [P, 2]), sbuf(st, "sd2", [P, 1])
        T = {n: sem("pr_" + n) for n in
             ("consts sub_land sub_ready sub_psum hsel_land hsel_free_pe hsel_free_act hT_psum hT_ready qp_psum "
              "qp_ready qT_psum qT_ready sc_psum sc_ready sc_free e_ready hcur_ready hcur_free dots_ready dots_free "
              "diag_ready diag_free f_psum f_free f_ready gx_ready gx_done g_ready var_ready sd_ready y_ready "
              "y_stored xres_land xres_free").split()}
        land = [sem(f"pr_land{s}") for s in range(RING)]
        slot_free = [sem(f"pr_slot_free{s}") for s in range(RING)]
        w_land = [sem(f"pr_w_land{n}") for n in range(4)]
        dve_c, act_c, pool_c = sem("pr_dve"), sem("pr_act"), sem("pr_pool")
        h2_t = h2_dram.rearrange("(t p) d -> p t d", p=P)
        x1_t = x1_dram.rearrange("(t p) d -> p t d", p=P)
        y_t = A["y_prompt"][0].rearrange("(t p) d -> p t d", p=P)
        uv = A["uv"]

        def run(eng, expert, select, finish=lambda t, c: None, tidy=lambda: None):
            def beside(t, before, after):
                for c in range(GROUPS):
                    expert(t, c)
                    if not isinstance(before, str):
                        finish(before, c)
                    if not isinstance(after, str):
                        select(after, c)
                tidy()

            def part_chosen(q):
                for c in (28, 29):
                    select(0, c, slice(q * PH // PARTS, (q + 1) * PH // PARTS))

            for c in range(16):
                select(0, c)
            part_chosen(0)
            for c in range(12):
                expert(0, c)
                select(0, 16 + c)
                if c % 4 == 3:
                    part_chosen(c // 4 + 1)
                for piece in BESIDE_FIRST.get(c, ()):
                    select(1, piece)
            for c in range(12, GROUPS):
                expert(0, c)
                for piece in BESIDE_FIRST.get(c, ()):
                    select(1, piece)
            tidy()
            with eng.Fori(1, TILES - 1) as t:
                beside(t, t - 1, t + 1)
            beside(TILES - 1, TILES - 2, None)
            beside(None, TILES - 1, "none")
            for c in range(GROUPS):
                finish(None, c)
            tidy()

        def enters(t, c):
            return c % (GROUPS // PARTS) == 0 if isinstance(t, int) and t == 0 else c == 0

        def index(t):
            return TILES if t is None else t

        def groups_of(t):
            return GROUPS // COPIES if t is None else GROUPS

        with nc.Block() as block:
            @block.sync
            def _(sp):
                sp.dma_start(qT[:], A["sub_keys"][0].rearrange("h q n d -> n (h q) d")).then_inc(T["sub_land"], 16)

                def select(t, c):
                    if c == 0:
                        take(sp, T["hsel_free_pe"])
                        take(sp, T["hsel_free_act"])
                        sp.dma_start(h_sel[:], flat(h2_t[:, ds(index(t), 1), :])).then_inc(T["hsel_land"], 16)

                def store(t):
                    take(sp, T["y_ready"])
                    if t is None:
                        sp.dma_start(A["y_sample"].rearrange("b t d -> (b t) d"), f[0:NS, :]).then_inc(T["y_stored"], 16)
                    else:
                        sp.dma_start(flat(y_t[:, ds(t, 1), :]), f[:]).then_inc(T["y_stored"], 16)

                def residual(t):
                    take(sp, T["xres_free"])
                    sp.dma_start(x_res[:], flat(x1_t[:, ds(index(t), 1), :])).then_inc(T["xres_land"], 16)

                select(0, 0)
                w_v = A["w_pq"][0].rearrange("(k p) n -> p k n", p=P)
                for n in range(4):
                    cols = slice(n * BANK, (n + 1) * BANK)
                    sp.dma_start(w[:, :, cols], w_v[:, :, cols]).then_inc(w_land[n], 16)
                select(1, 0)
                residual(0)
                with sp.Fori(0, TILES - 2) as i:
                    select(i + 2, 0)
                    store(i)
                    residual(i + 1)
                select(None, 0)
                store(TILES - 2)
                residual(TILES - 1)
                store(TILES - 1)
                residual(None)
                store(None)
                sp.wait_ge(T["y_stored"], 16)

            @block.gpsimd
            def _(pool):
                step = Steps(pool, pool_c)

                def expert(t, c):
                    if c >= groups_of(t):
                        return
                    if enters(t, c):
                        take(pool, T["e_ready"])
                    for s in range(GROUP):
                        take(pool, slot_free[(c * GROUP + s) % RING])
                        if s == 0:
                            src = e_all[:, ds(index(t), 1), c * GROUP:(c + 1) * GROUP]
                            step(nc.gpsimd.tensor_copy(stage[:, c % 4, :], flat(src)))
                            step.done()
                        slot = (c * GROUP + s) % RING
                        pool.indirect_dma_start(ring[:, slot, :], None, uv,
                                                bass.IndirectOffsetOnAxis(ap=stage[:, c % 4, s:s + 1], axis=0))\
                            .then_inc(land[slot], 16)
                run(pool, expert, lambda t, c, heads=ALL: None, tidy=step.reset)

            @block.tensor
            def _(pe):
                for s in range(RING):
                    pe.sem_inc(slot_free[s], 1)
                pe.sem_inc(T["hsel_free_pe"], 1)
                pe.sem_inc(T["diag_free"], 1)
                pe.sem_inc(T["f_free"], 1)
                pe.wait_ge(T["sub_land"], 16)
                for j in range(HP):
                    ins = nc.tensor.transpose(psum[:, 4 + j // 4, (j % 4) * PK:(j % 4 + 1) * PK], qT[:, j, :], ident[:])
                ins.then_inc(T["sub_psum"], 1)
                pe.wait_ge(T["sub_ready"], 1)

                def expert(t, c):
                    last = groups_of(t) - 1
                    if c > last:
                        return
                    if c == 0:
                        take(pe, T["f_free"])
                    for s in range(GROUP):
                        take(pe, T["diag_ready"])
                        slot = (c * GROUP + s) % RING
                        for n in range(2):
                            ins = nc.tensor.matmul(psum[:, n, :], diag[:, c % 2, s, :], ring[:, slot, D + n * BANK:D + (n + 1) * BANK],
                                                   start=(c == 0 and s == 0), stop=(c == last and s == GROUP - 1),
                                                   skip_group_check=True)
                            if n == 0 and s == 0:
                                ins.then_inc(T["diag_free"], 1)
                        ins.then_inc(T["f_psum"] if c == last and s == GROUP - 1 else slot_free[slot], 1)

                def select(t, c, heads=ALL):
                    if c == 0:
                        take(pe, T["hsel_land"], 16)
                        for k in range(KD):
                            ins = nc.tensor.transpose(psum[:, 2 + k // 4, (k % 4) * P:(k % 4 + 1) * P], h_sel[:, k * P:(k + 1) * P], ident[:])
                        ins.then_inc(T["hT_psum"], 1)
                    elif c <= 8:
                        n, half = (c - 1) // 2, (c - 1) % 2
                        if c == 1:
                            take(pe, T["hT_ready"])
                        if isinstance(t, int) and t == 0 and half == 0:
                            pe.wait_ge(w_land[n], 16)
                        for k in range(4 * half, 4 * half + 4):
                            ins = nc.tensor.matmul(psum[:, 4 + n, :], hT[:, k, :], w[:, k, n * BANK:(n + 1) * BANK],
                                                   start=(k == 0), stop=(k == KD - 1), skip_group_check=True)
                        if half:
                            ins.then_inc(T["qp_psum"], 1)
                    elif c in (9, 10):
                        if c == 9:
                            for n in range(4):
                                take(pe, T["qp_ready"])
                        else:
                            take(pe, T["qT_ready"])
                        for j in range(8):
                            hp = (c - 9) * 8 + j
                            ins = nc.tensor.transpose(psum[:, 2 + j // 4, (j % 4) * P:(j % 4 + 1) * P], sc[:, hp, :], ident[:])
                        ins.then_inc(T["qT_psum"], 1)
                    elif c == 11:
                        take(pe, T["qT_ready"])
                        for j in range(HP):
                            ins = nc.tensor.matmul(psum[:, 4 + j // 4, (j % 4) * PK:(j % 4 + 1) * PK], qT[:, j, :], subT[:, j, :],
                                                   start=True, stop=True)
                        ins.then_inc(T["sc_psum"], 1)
                run(pe, expert, select)

            @block.scalar
            def _(act):
                step = Steps(act, act_c)
                act.sem_inc(T["hsel_free_act"], 1)
                for j, name in enumerate(("ln2_g", "ln2_b")):
                    act.dma_start(lng[:, j], A[name].to_broadcast([P, D])).then_inc(T["consts"], 16)
                act.dma_start(fold[:], A["const_fold"]).then_inc(T["consts"], 16)
                act.dma_start(iota[:], A["const_iota"]).then_inc(T["consts"], 16)
                act.wait_ge(T["sub_psum"], 1)
                step(nc.scalar.copy(subT[:].rearrange("p j n -> p (j n)"), flat(psum[:, 4:8, :])))
                step.tell(T["sub_ready"])
                act.wait_ge(T["consts"], 4 * 16)
                step.reset()

                def expert(t, c):
                    last = groups_of(t) - 1
                    if c > last:
                        return
                    if c == 0:
                        take(act, T["hcur_free"])
                        step(nc.scalar.copy(h_cur[:], h_sel[:]))
                        step.tell(T["hcur_ready"], T["hsel_free_act"])
                    if enters(t, c):
                        take(act, T["g_ready"])
                    u = c % 2
                    take(act, T["dots_ready"])
                    step(nc.scalar.activation(act_g[:, u, :], dots[:, u, :], ACT.Gelu))
                    step.tell(T["dots_free"])
                    for s in range(GROUP):
                        k = c * GROUP + s
                        step(nc.scalar.activation(wgt[:, u, s:s + 1], act_g[:, u, s:s + 1], ACT.Copy,
                                                  scale=g_all[:, ds(index(t), 1), k:k + 1].rearrange("p a b -> p (a b)")))
                    step.done()
                    take(act, T["diag_free"])
                    for s in range(GROUP):
                        nc.scalar.activation(diag[:, u, s, :], (fold if t is None else ident)[:], ACT.Copy,
                                             scale=wgt[:, u, s:s + 1]).then_inc(T["diag_ready"], 1)
                    if c == last:
                        take(act, T["f_psum"])
                        act.sem_inc(slot_free[RING - 1], 1)
                        take(act, T["y_stored"], 16)
                        step(nc.scalar.copy(f[:], flat(psum[:, 0:2, :])))
                        step.tell(T["f_ready"], T["f_free"])

                def select(t, c, heads=ALL):
                    if c == 0:
                        take(act, T["hT_psum"])
                        act.sem_inc(T["hsel_free_pe"], 1)
                        step(nc.scalar.copy(hT[:].rearrange("p k n -> p (k n)"), flat(psum[:, 2:4, :])))
                        step.tell(T["hT_ready"])
                    elif c in (2, 4, 6, 8):
                        n = c // 2 - 1
                        if n == 0:
                            take(act, T["sc_free"])
                        take(act, T["qp_psum"])
                        step(nc.scalar.copy(sc[:, 4 * n:4 * n + 4, :].rearrange("p j n -> p (j n)"), psum[:, 4 + n, :]))
                        step.tell(T["qp_ready"])
                    elif c in (9, 10):
                        take(act, T["qT_psum"])
                        j = (c - 9) * 8
                        step(nc.scalar.copy(qT[:, j:j + 8, :].rearrange("p j n -> p (j n)"), flat(psum[:, 2:4, :])))
                        step.tell(T["qT_ready"])
                    elif c == 11:
                        take(act, T["sc_psum"])
                        step(nc.scalar.copy(sc[:].rearrange("p j n -> p (j n)"), flat(psum[:, 4:8, :])))
                        step.tell(T["sc_ready"])
                    elif c == 28:
                        take(act, T["gx_ready"])
                        step(nc.scalar.activation(cv[:, heads], cv[:, heads], ACT.Exp))
                        step.tell(T["gx_done"])

                def finish(t, c):
                    if c == 3:
                        take(act, T["var_ready"])
                        step(nc.scalar.activation(sd[:], ag[:, 1:2], ACT.Sqrt, bias=eps[:]))
                        step.tell(T["sd_ready"])

                act.sem_inc(T["y_stored"], 16)
                run(act, expert, select, finish, step.reset)

            @block.vector
            def _(dve):
                step = Steps(dve, dve_c)
                dve.wait_ge(T["consts"], 4 * 16)
                for n in ("hcur_free", "dots_free", "dots_free", "xres_free", "sc_free"):
                    dve.sem_inc(T[n], 1)

                def expert(t, c):
                    last = groups_of(t) - 1
                    if c > last:
                        return
                    if c == 0:
                        take(dve, T["hcur_ready"])
                    take(dve, T["dots_free"])
                    for s in range(GROUP):
                        k = c * GROUP + s
                        slot = k % RING
                        dve.wait_ge(land[slot], (index(t) * USES + (k // RING + 1)) * 16)
                        step(nc.vector.tensor_tensor_reduce(ring[:, slot, 0:D], ring[:, slot, 0:D], h_cur[:], 1.0, 0.0,
                                                            ALU.mult, ALU.add, dots[:, c % 2, s:s + 1]))
                    step.tell(T["dots_ready"])
                    if c == last:
                        dve.sem_inc(T["hcur_free"], 1)

                def best16(values, out, where):
                    for r in range(2):
                        o = slice(8 * r, 8 * r + 8)
                        for v, a, b in zip(values, out, where):
                            step(nc.vector.max(a[:, o], v))
                        step.done()
                        for v, a, b in zip(values, out, where):
                            step(nc.vector.max_index(b[:, o], a[:, o], v))
                        if r == 0:
                            step.done()
                            for v, a, b in zip(values, out, where):
                                step(nc.vector.match_replace(v, a[:, o], v, -3e38))
                        step.done()

                def select(t, c, heads=ALL):
                    if 12 <= c < 28:
                        h = (c - 12) // 2
                        if c == 12:
                            take(dve, T["sc_ready"])
                        if c % 2 == 0:
                            best16([sc[:, 2 * h + p, :] for p in range(2)], [sv[:, p] for p in range(2)], [si[:, p] for p in range(2)])
                            step(nc.vector.tensor_copy(sif[:], si[:]))
                            step(nc.vector.tensor_tensor(cand[:], over(sv[:, 0], TOPK),
                                                         sv[:, 1].unsqueeze(1).to_broadcast([P, TOPK, TOPK]), ALU.add))
                            step.done()
                            return
                        best16([cand[:].rearrange("p a b -> p (a b)")], [cv[:, h]], [ci])
                        step(nc.vector.tensor_scalar(cab[:, 0], ci[:], 4, None, ALU.logical_shift_right))
                        step(nc.vector.tensor_scalar(cab[:, 1], ci[:], TOPK - 1, None, ALU.bitwise_and))
                        step.done()
                        step(nc.vector.tensor_copy(cabf[:], cab[:]))
                        for p in range(2):
                            step.done()
                            step(nc.vector.tensor_tensor(hot[:], iota[:].unsqueeze(1).to_broadcast([P, TOPK, TOPK]), over(cabf[:, p], TOPK), ALU.is_equal))
                            step.done()
                            step(nc.vector.tensor_tensor(hot[:], hot[:], sif[:, p].unsqueeze(1).to_broadcast([P, TOPK, TOPK]), ALU.mult))
                            step.done()
                            step(nc.vector.tensor_reduce(eab[:, p, h], hot[:], AX, ALU.add))
                        step.done()
                        if c == 27:
                            dve.sem_inc(T["sc_free"], 1)
                    elif c == 28:
                        ef = [eab[:, p, heads].rearrange("p h k -> p (h k)") for p in range(2)]
                        ks = slice(heads.start * TOPK, heads.stop * TOPK)
                        if t is None:
                            for g in range(COPIES):
                                q, k = slice(g * NS, (g + 1) * NS), slice(g * NS, (g + 1) * NS)
                                step(nc.vector.scalar_tensor_tensor(out=e_all[q, TILES, 0:NS], in0=ef[0][q, k], scalar=float(PK),
                                                                    in1=ef[1][q, k], op0=ALU.mult, op1=ALU.add))
                        else:
                            step(nc.vector.scalar_tensor_tensor(out=flat(e_all[:, ds(t, 1), ks]), in0=ef[0], scalar=float(PK), in1=ef[1],
                                                                op0=ALU.mult, op1=ALU.add))
                        less, n = hot[:, heads, :], heads.stop - heads.start
                        step(nc.vector.tensor_tensor(less, cv[:, heads], cv[:, heads, 0:1].to_broadcast([P, n, TOPK]), ALU.subtract))
                        step.done()
                        step(nc.vector.tensor_copy(cv[:, heads], less))
                        step.tell(T["e_ready"], T["gx_ready"])
                    elif c == 29:
                        take(dve, T["gx_done"])
                        step(nc.vector.tensor_reduce(gsum[:, heads], cv[:, heads], AX, ALU.add))
                        step.done()
                        step(nc.vector.reciprocal(gsum[:, heads], gsum[:, heads]))
                        step.done()
                        if t is None:
                            step(nc.vector.tensor_tensor(cv[:], cv[:], over(gsum[:], TOPK), ALU.mult))
                            step.done()
                            gf = cv[:].rearrange("p h k -> p (h k)")
                            for g in range(COPIES):
                                q = slice(g * NS, (g + 1) * NS)
                                step(nc.vector.tensor_copy(g_all[q, TILES, 0:NS], gf[q, q]))
                        else:
                            ks = slice(heads.start * TOPK, heads.stop * TOPK)
                            dst = flat(g_all[:, ds(t, 1), ks]).rearrange("p (h k) -> p h k", k=TOPK)
                            step(nc.vector.tensor_tensor(dst, cv[:, heads], over(gsum[:, heads], TOPK), ALU.mult))
                        step.tell(T["g_ready"])

                def finish(t, c):
                    if c == 2:
                        take(dve, T["f_ready"])
                        step(nc.vector.tensor_tensor(f[:], f[:], gate2[:, int(t is None)], ALU.mult))
                        take(dve, T["xres_land"], 16)
                        step.done()
                        step(nc.vector.scalar_tensor_tensor(out=f[:], in0=x_res[:], scalar=ALPHA, in1=f[:], op0=ALU.mult, op1=ALU.add))
                        step.tell(T["xres_free"])
                        for b in range(2):
                            step(nc.vector.bn_stats(bn[:, b, :], f[:, b * BANK:(b + 1) * BANK]))
                        step.done()
                        step(nc.vector.bn_aggr(ag[:], bn[:].rearrange("p a b -> p (a b)")))
                        step.tell(T["var_ready"])
                    elif c == 4:
                        take(dve, T["sd_ready"])
                        step(nc.vector.reciprocal(sd[:], sd[:]))
                        step.done()
                        step(nc.vector.tensor_scalar(f[:], f[:], ag[:, 0:1], sd[:], ALU.subtract, ALU.mult))
                        step.done()
                        step(nc.vector.tensor_tensor(f[:], f[:], lng[:, 0], ALU.mult))
                        step.done()
                        step(nc.vector.tensor_tensor(f[:], f[:], lng[:, 1], ALU.add))
                        step.tell(T["y_ready"])

                run(dve, expert, select, finish, step.reset)


_INS = ['x_prompt', 'x_sample', 'cache_k', 'cache_v', 'state_conv', 'page_table', 'c_prompt', 'c_sample', 'rel_bias',
        'w_ada', 'b_ada', 'w_in', 'lambda_q1', 'lambda_k1', 'lambda_q2', 'lambda_k2', 'subln_w', 'conv_w', 'w_out',
        'ln1_g', 'ln1_b', 'w_pq', 'sub_keys', 'ln2_g', 'ln2_b']
_OUTS = {'y_prompt': (1, SEQ, D), 'y_sample': (NB, NT, D), 'new_k_prompt': (1, 1, SEQ, H, 2, DH),
         'new_v_prompt': (1, 1, SEQ, H, DV), 'new_conv_prompt': (1, 1, 2, AW), 'new_k_sample': (1, NB, NT, H, 2, DH),
         'new_v_sample': (1, NB, NT, H, DV), 'new_conv_sample': (1, NB, 2, AW)}


def shape_constants():
    def hot(dist):
        n = np.maximum(dist, 0)
        exact = BUCKETS // 2
        large = exact + (np.log(np.maximum(n, exact).astype(np.float32) / np.float32(exact)) / np.float32(math.log(MAX_DIST / exact))
                         * np.float32(BUCKETS - exact)).astype(np.int32)
        bucket = np.where(n < exact, n, np.minimum(large, BUCKETS - 1))
        bucket = np.where(dist < 0, BUCKETS, bucket)
        return (np.arange(BUCKETS + 1)[(slice(None),) + (None,) * dist.ndim] == bucket).astype(np.float32)

    onehot = hot(SEQ + P - 1 - np.arange(TOEP))
    tail = hot(P + np.arange(NT)[:, None] - np.arange(TAIL)[None, :])
    far = hot(np.full((NT, 1), PAST))
    R = H * 2 * NT
    r = np.arange(R)
    head, second, token = r // (2 * NT), (r // NT) % 2, r % NT
    mask = (head[:, None] == np.arange(AW)[None, :] // DV)
    comb = token[:, None, None] + NT * np.arange(NB)[None, :, None] == np.arange(NS)[None, None, :]
    rows = np.concatenate([(second == 0)[:, None], (second == 1)[:, None], mask, comb.reshape(R, NB * NS)], 1).astype(np.float32)
    p = np.arange(P)
    return {
        'const_ident': np.eye(P, dtype=np.float32),
        'const_fold': (p[:, None] % NS == p[None, :] % NS).astype(np.float32),
        'const_onehot': onehot,
        'const_tail': np.concatenate([tail, far], 2).astype(np.float32),
        'const_rows': rows,
        'const_iota': np.broadcast_to(np.arange(TOPK, dtype=np.float32), (P, TOPK)).copy(),
    }


def kernel(**inputs):
    import numpy as _np
    import concourse.bacc as _bacc
    from concourse import mybir as _mybir
    from concourse.bass_utils import run_bass_kernel_spmd as _run

    nc = _bacc.Bacc("TRN2", target_bir_lowering=False, num_devices=1)
    arrays = {name: _np.ascontiguousarray(inputs[name]) for name in _INS}
    arrays['uv'] = _np.concatenate([_np.asarray(inputs['peer_u'])[0], _np.asarray(inputs['peer_v'])[0]], axis=1)
    arrays |= shape_constants()
    A = {}
    for name, a in arrays.items():
        A[name] = nc.dram_tensor(f"in_{name}", a.shape, _mybir.dt.from_np(a.dtype), kind="ExternalInput").ap()
    for name, shape in _OUTS.items():
        A[name] = nc.dram_tensor(f"out_{name}", shape, _mybir.dt.float32, kind="ExternalOutput").ap()
    build(nc, A)
    r = _run(nc, [{f"in_{name}": a for name, a in arrays.items()}], core_ids=[0])
    return tuple(r.results[0][f"out_{name}"] for name in _OUTS)
```
